# Optimizing a Trainium2 kernel written in Bass

```python
import jax, jax.numpy as jnp
from jax import lax
import numpy as np

D_MODEL = 1024
BATCH = 1
SEQ = 256
DEPTH = 1

MEM_LEN = 256
EPS = 1e-6

M_HEADS = 4
M_DV = D_MODEL // 8
M_DQK = M_DV // 2
M_CONV = 4
M_CHUNK = 64

A_HEADS = 8
A_KV_HEADS = 2
A_DH = 64
WINDOW = 128
A_BLOCK = 128

X_HEADS = 4
X_DH = D_MODEL // X_HEADS

P_HEADS = 8
P_NKEYS = 128
P_EXPERTS = P_NKEYS * P_NKEYS
P_KEY_DIM = 128
P_TOPK = 16
P_TOKEN_BLOCK = 128

IN_SIZES = (M_HEADS * M_DQK, M_HEADS * M_DQK, M_HEADS * M_DV, M_HEADS * M_DV, M_HEADS, M_HEADS,
            A_HEADS * A_DH, A_KV_HEADS * A_DH, A_KV_HEADS * A_DH)
P_IN = sum(IN_SIZES)
MIX_WIDTH = M_HEADS * M_DV + A_HEADS * A_DH


def rmsnorm(x, g):
    xf = x.astype(jnp.float32)
    y = xf * lax.rsqrt(jnp.mean(xf * xf, axis=-1, keepdims=True) + EPS)
    return (y * g.astype(jnp.float32)).astype(x.dtype)

def causal_depthwise_conv(x, w, b):
    y = lax.conv_general_dilated(
        x, w[:, None, :].astype(x.dtype), window_strides=(1,),
        padding=[(w.shape[0] - 1, 0)], dimension_numbers=('NWC', 'WIO', 'NWC'),
        feature_group_count=x.shape[-1])
    return y + b.astype(x.dtype)

def mlstm_chunkwise(q, k, v, i_pre, f_pre):
    B, S, H, _ = q.shape
    L = M_CHUNK
    nc = S // L
    f32 = jnp.float32

    def chunks(t):
        t = t.astype(f32).reshape((B, nc, L, H) + t.shape[3:])
        return jnp.moveaxis(t, (1, 3), (0, 2))

    qc = chunks(q) * (M_DQK ** -0.5)
    kc = chunks(k)
    vc = chunks(v)
    ic = chunks(i_pre)
    lfc = chunks(jax.nn.log_sigmoid(f_pre.astype(f32)))
    causal = jnp.tril(jnp.ones((L, L), dtype=bool))

    def step(carry, inp):
        C, n, m = carry
        qb, kb, vb, ib, lfb = inp
        b = jnp.cumsum(lfb, axis=-1)
        log_d = jnp.where(causal, b[..., :, None] - b[..., None, :] + ib[..., None, :], -jnp.inf)
        inter = b + m[..., None]
        m_t = jnp.maximum(inter, jnp.max(log_d, axis=-1))
        d = jnp.exp(log_d - m_t[..., None])
        s = jnp.einsum('bhtk,bhsk->bhts', qb, kb) * d
        w_inter = jnp.exp(inter - m_t)
        num = jnp.einsum('bhts,bhsv->bhtv', s, vb) + w_inter[..., None] * jnp.einsum('bhvk,bhtk->bhtv', C, qb)
        den = jnp.sum(s, axis=-1) + w_inter * jnp.einsum('bhk,bhtk->bht', n, qb)
        h = num / jnp.maximum(jnp.abs(den), jnp.exp(-m_t))[..., None]
        m_new = m_t[..., -1]
        w = jnp.exp(b[..., -1:] - b + ib - m_new[..., None])
        decay = jnp.exp(b[..., -1] + m - m_new)
        C_new = decay[..., None, None] * C + jnp.einsum('bhs,bhsv,bhsk->bhvk', w, vb, kb)
        n_new = decay[..., None] * n + jnp.einsum('bhs,bhsk->bhk', w, kb)
        return (C_new, n_new, m_new), h

    init = (jnp.zeros((B, H, M_DV, M_DQK), f32), jnp.zeros((B, H, M_DQK), f32), jnp.zeros((B, H), f32))
    _, h = lax.scan(step, init, (qc, kc, vc, ic, lfc))
    h = jnp.moveaxis(h, (0, 2), (1, 3)).reshape(B, S, H, M_DV)
    return h.astype(v.dtype)

def sliding_window_gqa_sinks(q, k, v, sinks):
    B, S, Hq, dh = q.shape
    Hkv = k.shape[2]
    G = Hq // Hkv
    nb = S // A_BLOCK
    f32 = jnp.float32
    qb = q.astype(f32).reshape(B, nb, A_BLOCK, Hkv, G, dh)

    def band_blocks(t):
        t = t.astype(f32)
        prev = jnp.concatenate([jnp.zeros_like(t[:, :A_BLOCK]), t[:, :S - A_BLOCK]], axis=1)
        return jnp.concatenate([prev.reshape(B, nb, A_BLOCK, Hkv, dh),
                                t.reshape(B, nb, A_BLOCK, Hkv, dh)], axis=2)

    kb = band_blocks(k)
    vb = band_blocks(v)
    qi = jnp.arange(A_BLOCK)[:, None]
    kj = jnp.arange(2 * A_BLOCK)[None, :]
    diff = qi - kj + A_BLOCK
    band = (diff >= 0) & (diff < WINDOW)
    exists = (jnp.arange(nb)[:, None, None] > 0) | (kj >= A_BLOCK)[None]
    mask = band[None] & exists

    scores = jnp.einsum('bnqhgd,bnkhd->bnhgqk', qb, kb) * (dh ** -0.5)
    scores = jnp.where(mask[None, :, None, None], scores, -jnp.inf)
    sink = sinks.astype(f32).reshape(Hkv, G)[None, None, :, :, None, None]
    mx = jnp.maximum(jnp.max(scores, axis=-1, keepdims=True), sink)
    p = jnp.exp(scores - mx)
    probs = p / (jnp.sum(p, axis=-1, keepdims=True) + jnp.exp(sink - mx))
    out = jnp.einsum('bnhgqk,bnkhd->bnqhgd', probs, vb)
    return out.reshape(B, S, Hq * dh).astype(q.dtype)

def memory_cross_attention(xn, memn, w_q, w_k, w_v, w_o):
    B, S, D = xn.shape
    M = memn.shape[1]
    f32 = jnp.float32
    q = (xn @ w_q).reshape(B, S, X_HEADS, X_DH).astype(f32)
    k = (memn @ w_k).reshape(B, M, X_HEADS, X_DH).astype(f32)
    v = (memn @ w_v).reshape(B, M, X_HEADS, X_DH).astype(f32)
    p = jax.nn.softmax(jnp.einsum('bshd,bmhd->bhsm', q, k) * (X_DH ** -0.5), axis=-1)
    o = jnp.einsum('bhsm,bmhd->bshd', p, v).reshape(B, S, X_HEADS * X_DH).astype(xn.dtype)
    return o @ w_o

def peer_ffn(xn, w_pq, sub_keys1, sub_keys2, expert_down, expert_up):
    B, S, D = xn.shape
    T = P_TOKEN_BLOCK
    xt = xn.reshape(-1, T, D)

    def block(xb):
        qh = (xb @ w_pq).reshape(T, P_HEADS, 2, P_KEY_DIM).astype(jnp.float32)
        s1 = jnp.einsum('thd,nd->thn', qh[:, :, 0], sub_keys1.astype(jnp.float32))
        s2 = jnp.einsum('thd,nd->thn', qh[:, :, 1], sub_keys2.astype(jnp.float32))
        v1, i1 = lax.top_k(s1, P_TOPK)
        v2, i2 = lax.top_k(s2, P_TOPK)
        cand_s = (v1[..., :, None] + v2[..., None, :]).reshape(T, P_HEADS, P_TOPK * P_TOPK)
        cand_i = (i1[..., :, None] * P_NKEYS + i2[..., None, :]).reshape(T, P_HEADS, P_TOPK * P_TOPK)
        top_s, pos = lax.top_k(cand_s, P_TOPK)
        eidx = jnp.take_along_axis(cand_i, pos, axis=-1)
        g = jax.nn.softmax(top_s, axis=-1)
        u = expert_down[eidx]
        a = jax.nn.gelu(jnp.einsum('thkd,td->thk', u, xb), approximate=False)
        coef = (g * a.astype(jnp.float32)).astype(xb.dtype)
        return jnp.einsum('thk,thkd->td', coef, expert_up[eidx])

    return lax.map(block, xt).reshape(B, S, D)

def first_inputs(seed: int = 0) -> dict:
    key = jax.random.key(seed)
    ks = jax.random.split(key, 24)
    f32 = jnp.float32

    def nrm(k, shape, scale):
        return jax.random.normal(k, shape, f32) * scale

    Dn = D_MODEL ** -0.5
    qk_ch = 2 * M_HEADS * M_DQK
    return {
        "x": nrm(ks[0], (BATCH, SEQ, D_MODEL), 1.0),
        "mem": nrm(ks[1], (BATCH, MEM_LEN, D_MODEL), 1.0),
        "g_mix": 1.0 + nrm(ks[2], (DEPTH, D_MODEL), 0.02),
        "w_in": nrm(ks[3], (DEPTH, D_MODEL, P_IN), Dn),
        "conv_w": nrm(ks[4], (DEPTH, M_CONV, qk_ch), M_CONV ** -0.5),
        "conv_b": nrm(ks[5], (DEPTH, qk_ch), 0.02),
        "b_igate": nrm(ks[6], (DEPTH, M_HEADS), 0.1),
        "b_fgate": jnp.linspace(3.0, 6.0, M_HEADS, dtype=f32)[None] + nrm(ks[7], (DEPTH, M_HEADS), 0.1),
        "g_mhead": 1.0 + nrm(ks[8], (DEPTH, M_HEADS * M_DV), 0.02),
        "sinks": nrm(ks[9], (DEPTH, A_HEADS), 0.5),
        "w_out": nrm(ks[10], (DEPTH, MIX_WIDTH, D_MODEL), MIX_WIDTH ** -0.5),
        "g_cross": 1.0 + nrm(ks[11], (DEPTH, D_MODEL), 0.02),
        "g_mem": 1.0 + nrm(ks[12], (DEPTH, D_MODEL), 0.02),
        "w_xq": nrm(ks[13], (DEPTH, D_MODEL, X_HEADS * X_DH), Dn),
        "w_xk": nrm(ks[14], (DEPTH, D_MODEL, X_HEADS * X_DH), Dn),
        "w_xv": nrm(ks[15], (DEPTH, D_MODEL, X_HEADS * X_DH), Dn),
        "w_xo": nrm(ks[16], (DEPTH, X_HEADS * X_DH, D_MODEL), (X_HEADS * X_DH) ** -0.5),
        "g_ffn": 1.0 + nrm(ks[17], (DEPTH, D_MODEL), 0.02),
        "w_pq": nrm(ks[18], (DEPTH, D_MODEL, P_HEADS * 2 * P_KEY_DIM), Dn),
        "sub_keys1": nrm(ks[19], (DEPTH, P_NKEYS, P_KEY_DIM), P_KEY_DIM ** -0.5),
        "sub_keys2": nrm(ks[20], (DEPTH, P_NKEYS, P_KEY_DIM), P_KEY_DIM ** -0.5),
        "expert_down": nrm(ks[21], (DEPTH, P_EXPERTS, D_MODEL), Dn),
        "expert_up": nrm(ks[22], (DEPTH, P_EXPERTS, D_MODEL), Dn),
        "g_final": 1.0 + nrm(ks[23], (D_MODEL,), 0.02),
    }

def first_block(x, mem, g_mix, w_in, conv_w, conv_b, b_igate, b_fgate, g_mhead, sinks, w_out,
              g_cross, g_mem, w_xq, w_xk, w_xv, w_xo, g_ffn, w_pq, sub_keys1, sub_keys2,
              expert_down, expert_up, g_final):
    B, S, _ = x.shape
    split_points = [int(c) for c in np.cumsum(IN_SIZES)[:-1]]
    h = x
    for l in range(DEPTH):
        xn = rmsnorm(h, g_mix[l])
        proj = xn @ w_in[l]
        mq, mk, mv, mo, mi, mf, aq, ak, av = jnp.split(proj, split_points, axis=-1)
        qk = jax.nn.silu(causal_depthwise_conv(jnp.concatenate([mq, mk], axis=-1), conv_w[l], conv_b[l]))
        mq, mk = jnp.split(qk, 2, axis=-1)
        hm = mlstm_chunkwise(mq.reshape(B, S, M_HEADS, M_DQK), mk.reshape(B, S, M_HEADS, M_DQK),
                             mv.reshape(B, S, M_HEADS, M_DV),
                             mi + b_igate[l].astype(mi.dtype), mf + b_fgate[l].astype(mf.dtype))
        hm = rmsnorm(hm, g_mhead[l].reshape(M_HEADS, M_DV)).reshape(B, S, M_HEADS * M_DV)
        hm = (jax.nn.sigmoid(mo) * hm).astype(x.dtype)
        ha = sliding_window_gqa_sinks(aq.reshape(B, S, A_HEADS, A_DH), ak.reshape(B, S, A_KV_HEADS, A_DH),
                                      av.reshape(B, S, A_KV_HEADS, A_DH), sinks[l])
        h = h + jnp.concatenate([hm, ha], axis=-1) @ w_out[l]
        h = h + memory_cross_attention(rmsnorm(h, g_cross[l]), rmsnorm(mem, g_mem[l]),
                                       w_xq[l], w_xk[l], w_xv[l], w_xo[l])
        h = h + peer_ffn(rmsnorm(h, g_ffn[l]), w_pq[l], sub_keys1[l], sub_keys2[l],
                         expert_down[l], expert_up[l])
    return rmsnorm(h, g_final)


PLE_DIM = 256
GLA_HEADS = 4
GLA_DK = D_MODEL // 8
GLA_DV = D_MODEL // 4
GLA_GATE_RANK = 16
GLA_GATE_TAU = 16.0
GLA_CHUNK = 64
MOBA_HEADS = 8
MOBA_DH = D_MODEL // 8
MOBA_BLOCK = 256
MOBA_TOPK = 3
MOBA_QCHUNK = 32
D_FF = 4 * D_MODEL

IN_SPLITS = (
    GLA_HEADS * GLA_DK,
    GLA_HEADS * GLA_DK,
    GLA_HEADS * GLA_DV,
    GLA_GATE_RANK,
    GLA_HEADS * GLA_DV,
    MOBA_HEADS * MOBA_DH,
    MOBA_HEADS * MOBA_DH,
    MOBA_HEADS * MOBA_DH,
    D_MODEL,
    D_MODEL,
)
N_IN = sum(IN_SPLITS)


def rms_norm(x, g):
    xf = x.astype(jnp.float32)
    y = xf * lax.rsqrt(jnp.mean(xf * xf, axis=-1, keepdims=True) + EPS)
    return (y * g.astype(jnp.float32)).astype(x.dtype)

def gla_chunked(q, k, v, log_a):
    B, S, H, dk = q.shape
    dv = v.shape[-1]
    n = S // GLA_CHUNK

    def chunk(t):
        return t.astype(jnp.float32).reshape(B, n, GLA_CHUNK, H, t.shape[-1]).transpose(0, 3, 1, 2, 4)

    q, k, v, log_a = chunk(q), chunk(k), chunk(v), chunk(log_a)
    b = jnp.cumsum(log_a, axis=3)
    b_last = b[:, :, :, -1:, :]
    qd = q * jnp.exp(b) * (dk ** -0.5)
    kd = k * jnp.exp(-b)
    kl = k * jnp.exp(b_last - b)
    kv = jnp.einsum('bhncd,bhnce->bhnde', kl, v)
    decay = jnp.exp(b_last[:, :, :, 0, :])

    def step(state, inp):
        dec, kv_n = inp
        return dec[..., None] * state + kv_n, state

    s0 = jnp.zeros((B, H, dk, dv), jnp.float32)
    _, s_prev = lax.scan(step, s0, (jnp.moveaxis(decay, 2, 0), jnp.moveaxis(kv, 2, 0)))
    s_prev = jnp.moveaxis(s_prev, 0, 2)
    o_inter = jnp.einsum('bhncd,bhnde->bhnce', qd, s_prev)
    causal = jnp.tril(jnp.ones((GLA_CHUNK, GLA_CHUNK), bool))
    a = jnp.where(causal, jnp.einsum('bhncd,bhnsd->bhncs', qd, kd), 0.0)
    o = o_inter + jnp.einsum('bhncs,bhnse->bhnce', a, v)
    return o.transpose(0, 2, 3, 1, 4).reshape(B, S, H, dv)

def moba_attention(q, k, v):
    B, S, H, dh = q.shape
    s_pad = -(-S // MOBA_BLOCK) * MOBA_BLOCK
    nb = s_pad // MOBA_BLOCK
    n_sel = min(MOBA_TOPK, max(nb - 1, 1))
    nq = s_pad // MOBA_QCHUNK
    pad = ((0, 0), (0, s_pad - S), (0, 0), (0, 0))
    q, k, v = [jnp.pad(t, pad).transpose(0, 2, 1, 3) for t in (q, k, v)]
    kb = k.reshape(B, H, nb, MOBA_BLOCK, dh)
    vb = v.reshape(B, H, nb, MOBA_BLOCK, dh)
    scale = dh ** -0.5
    slopes = 2.0 ** (-8.0 * jnp.arange(1, H + 1, dtype=jnp.float32) / H)

    k_mean = jnp.mean(kb.astype(jnp.float32), axis=3)
    gate = jnp.einsum('bhsd,bhnd->bhsn', q.astype(jnp.float32), k_mean)
    pos = jnp.arange(s_pad)
    fully_past = jnp.arange(nb)[None, :] < (pos // MOBA_BLOCK)[:, None]
    gate = jnp.where(fully_past, gate, -jnp.inf)
    top_val, top_idx = lax.top_k(gate, n_sel)
    valid = jnp.isfinite(top_val)

    def to_chunks(t):
        return jnp.moveaxis(t.reshape(B, H, nq, MOBA_QCHUNK, *t.shape[3:]), 2, 0)

    b_ix = jnp.arange(B)[:, None, None, None]
    h_ix = jnp.arange(H)[None, :, None, None]

    def attend(args):
        q_c, idx_c, valid_c, c = args
        t = c * MOBA_QCHUNK + jnp.arange(MOBA_QCHUNK)
        blk = (c * MOBA_QCHUNK) // MOBA_BLOCK
        k_own = lax.dynamic_index_in_dim(kb, blk, axis=2, keepdims=False)
        v_own = lax.dynamic_index_in_dim(vb, blk, axis=2, keepdims=False)
        own_pos = blk * MOBA_BLOCK + jnp.arange(MOBA_BLOCK)
        d_own = (t[:, None] - own_pos[None, :]).astype(jnp.float32)
        sc_own = (jnp.einsum('bhqd,bhkd->bhqk', q_c, k_own).astype(jnp.float32) * scale
                  - slopes[:, None, None] * jnp.abs(d_own))
        sc_own = jnp.where(d_own >= 0, sc_own, -jnp.inf)
        k_sel = kb[b_ix, h_ix, idx_c]
        v_sel = vb[b_ix, h_ix, idx_c]
        sel_pos = idx_c[..., None] * MOBA_BLOCK + jnp.arange(MOBA_BLOCK)
        d_sel = (t[:, None, None] - sel_pos).astype(jnp.float32)
        sc_sel = (jnp.einsum('bhqd,bhqnkd->bhqnk', q_c, k_sel).astype(jnp.float32) * scale
                  - slopes[:, None, None, None] * jnp.abs(d_sel))
        sc_sel = jnp.where(valid_c[..., None], sc_sel, -jnp.inf)
        scores = jnp.concatenate(
            [sc_own, sc_sel.reshape(B, H, MOBA_QCHUNK, n_sel * MOBA_BLOCK)], axis=-1)
        prob = jax.nn.softmax(scores, axis=-1).astype(v.dtype)
        p_own = prob[..., :MOBA_BLOCK]
        p_sel = prob[..., MOBA_BLOCK:].reshape(B, H, MOBA_QCHUNK, n_sel, MOBA_BLOCK)
        return (jnp.einsum('bhqk,bhkd->bhqd', p_own, v_own)
                + jnp.einsum('bhqnk,bhqnkd->bhqd', p_sel, v_sel))

    out = lax.map(attend, (to_chunks(q), to_chunks(top_idx), to_chunks(valid), jnp.arange(nq)))
    out = jnp.moveaxis(out, 0, 2).reshape(B, H, s_pad, dh)[:, :, :S]
    return out.transpose(0, 2, 1, 3).reshape(B, S, H * dh)

def second_inputs(seed: int = 0) -> dict:
    key = jax.random.key(seed)
    ks = jax.random.split(key, 20)

    def nrm(k, shape, fan_in, scale=1.0):
        return jax.random.normal(k, shape, jnp.float32) * (scale * fan_in ** -0.5)

    def gain(k, shape):
        return 1.0 + 0.05 * jax.random.normal(k, shape, jnp.float32)

    return {
        'x': jax.random.normal(ks[0], (BATCH, SEQ, D_MODEL), jnp.float32),
        'p': jax.random.normal(ks[1], (DEPTH, BATCH, SEQ, PLE_DIM), jnp.float32),
        'norm_mix': gain(ks[2], (DEPTH, D_MODEL)),
        'w_in': nrm(ks[3], (DEPTH, D_MODEL, N_IN), D_MODEL),
        'gla_gate_w2': nrm(ks[4], (DEPTH, GLA_GATE_RANK, GLA_HEADS * GLA_DK), GLA_GATE_RANK),
        'gla_gate_b': 0.1 * jax.random.normal(ks[5], (DEPTH, GLA_HEADS * GLA_DK), jnp.float32),
        'gla_out_norm': gain(ks[6], (DEPTH, GLA_HEADS, GLA_DV)),
        'moba_q_norm': gain(ks[7], (DEPTH, MOBA_DH)),
        'moba_k_norm': gain(ks[8], (DEPTH, MOBA_DH)),
        'w_branch_a': nrm(ks[9], (DEPTH, GLA_HEADS * GLA_DV, D_MODEL), GLA_HEADS * GLA_DV),
        'w_branch_b': nrm(ks[10], (DEPTH, MOBA_HEADS * MOBA_DH, D_MODEL), MOBA_HEADS * MOBA_DH),
        'w_out': nrm(ks[11], (DEPTH, D_MODEL, D_MODEL), D_MODEL, 0.5),
        'norm_mlp': gain(ks[12], (DEPTH, D_MODEL)),
        'w_up': nrm(ks[13], (DEPTH, D_MODEL, D_FF), D_MODEL),
        'w_down': nrm(ks[14], (DEPTH, D_FF, D_MODEL), D_FF, 0.5),
        'norm_ple': gain(ks[15], (DEPTH, D_MODEL)),
        'w_ple_gate': nrm(ks[16], (DEPTH, D_MODEL, D_MODEL), D_MODEL),
        'w_ple': nrm(ks[17], (DEPTH, PLE_DIM, D_MODEL), PLE_DIM, 0.5),
    }

def second_block(x, p, norm_mix, w_in, gla_gate_w2, gla_gate_b, gla_out_norm, moba_q_norm,
              moba_k_norm, w_branch_a, w_branch_b, w_out, norm_mlp, w_up, w_down,
              norm_ple, w_ple_gate, w_ple):
    B, S, _ = x.shape
    points = []
    acc = 0
    for sz in IN_SPLITS[:-1]:
        acc += sz
        points.append(acc)

    for i in range(DEPTH):
        h = rms_norm(x, norm_mix[i])
        u = h @ w_in[i]
        (gq, gk, gv, g_lr, g_r, mq, mk, mv, gate_a, gate_b) = jnp.split(u, points, axis=-1)

        z = (g_lr @ gla_gate_w2[i] + gla_gate_b[i]).astype(jnp.float32)
        log_a = jax.nn.log_sigmoid(z) / GLA_GATE_TAU
        o_a = gla_chunked(gq.reshape(B, S, GLA_HEADS, GLA_DK),
                          gk.reshape(B, S, GLA_HEADS, GLA_DK),
                          gv.reshape(B, S, GLA_HEADS, GLA_DV),
                          log_a.reshape(B, S, GLA_HEADS, GLA_DK)).astype(x.dtype)
        o_a = rms_norm(o_a, gla_out_norm[i]).reshape(B, S, GLA_HEADS * GLA_DV) * jax.nn.silu(g_r)
        y_a = o_a @ w_branch_a[i]

        qh = rms_norm(mq.reshape(B, S, MOBA_HEADS, MOBA_DH), moba_q_norm[i])
        kh = rms_norm(mk.reshape(B, S, MOBA_HEADS, MOBA_DH), moba_k_norm[i])
        vh = mv.reshape(B, S, MOBA_HEADS, MOBA_DH)
        y_b = moba_attention(qh, kh, vh) @ w_branch_b[i]

        y = jax.nn.sigmoid(gate_a) * y_a + jax.nn.sigmoid(gate_b) * y_b
        x = x + y @ w_out[i]

        h2 = rms_norm(x, norm_mlp[i])
        x = x + jnp.square(jax.nn.relu(h2 @ w_up[i])) @ w_down[i]

        ple_gate = jax.nn.sigmoid(rms_norm(x, norm_ple[i]) @ w_ple_gate[i])
        x = x + ple_gate * (p[i] @ w_ple[i])
    return x


def setup_inputs(seed=0):
    out = dict(first_inputs(seed))
    for name, value in second_inputs(seed + 1).items():
        if name != "x":
            out[name + "_2"] = value
    return out


def reference(
    x, mem, g_mix, w_in, conv_w, conv_b, b_igate, b_fgate, g_mhead, sinks, w_out, g_cross,
    g_mem, w_xq, w_xk, w_xv, w_xo, g_ffn, w_pq, sub_keys1, sub_keys2, expert_down, expert_up,
    g_final, p_2, norm_mix_2, w_in_2, gla_gate_w2_2, gla_gate_b_2, gla_out_norm_2,
    moba_q_norm_2, moba_k_norm_2, w_branch_a_2, w_branch_b_2, w_out_2, norm_mlp_2, w_up_2,
    w_down_2, norm_ple_2, w_ple_gate_2, w_ple_2,
):
    x = first_block(
        x, mem, g_mix, w_in, conv_w, conv_b, b_igate, b_fgate, g_mhead, sinks, w_out, g_cross,
        g_mem, w_xq, w_xk, w_xv, w_xo, g_ffn, w_pq, sub_keys1, sub_keys2, expert_down,
        expert_up, g_final,
    )
    return second_block(
        x, p_2, norm_mix_2, w_in_2, gla_gate_w2_2, gla_gate_b_2, gla_out_norm_2, moba_q_norm_2,
        moba_k_norm_2, w_branch_a_2, w_branch_b_2, w_out_2, norm_mlp_2, w_up_2, w_down_2,
        norm_ple_2, w_ple_gate_2, w_ple_2,
    )


_drawn_inputs = setup_inputs


def setup_inputs(seed=0):
    import zlib

    import numpy as np

    out = dict(_drawn_inputs(seed))
    spreads = {}
    factors = {'g_mix': 3.775,
     'conv_b': 5.956,
     'b_igate': 200.0,
     'g_mhead': 7.543,
     'sinks': 6.415,
     'g_cross': 8.0,
     'g_mem': 8.0,
     'g_ffn': 8.0,
     'w_pq': 3.794,
     'sub_keys1': 3.843,
     'sub_keys2': 3.874,
     'expert_down': 4.24,
     'expert_up': 3.765,
     'g_final': 2.697,
     'norm_mix_2': 3.126,
     'gla_gate_b_2': 7.831,
     'gla_out_norm_2': 7.355,
     'moba_q_norm_2': 8.0,
     'moba_k_norm_2': 8.0,
     'norm_ple_2': 200.0,
     'norm_mlp_2': 8.0,
     'p_2': 6.369,
     'w_ple_gate_2': 8.0,
     'w_ple_2': 6.352}
    for name, (base, spread) in spreads.items():
        noise = np.random.default_rng([zlib.crc32(name.encode()), seed]).standard_normal(out[name].shape)
        drawn = base * np.exp(spread * noise) if base else spread * noise
        out[name] = __import__('jax').numpy.asarray(drawn.astype(out[name].dtype))
    for name, factor in factors.items():
        out[name] = (out[name] * factor).astype(out[name].dtype)
    return out
```

```python
from collections import deque
from contextlib import ExitStack

import numpy as np

import concourse.bass as bass
from concourse import mybir

F32 = mybir.dt.float32
F32R = mybir.dt.float32r
I32 = mybir.dt.int32
U32 = mybir.dt.uint32
ALU = mybir.AluOpType
ACT = mybir.ActivationFunctionType
AX = mybir.AxisListType.X

EPS = 1e-6
NEG = -1e30
RING = 4
NHL = 2

TILES = [("akv", 1, "f"), ("qk", 1, "f"), ("aq", 1, "f"), ("mv", 1, "t"), ("mo", 1, "t"), ("wo1", 2, "t"), ("xq", 2, "f"),
         ("xk", 2, "f"), ("xv", 2, "t"), ("xo", 2, "t"), ("pq", 4, "f"), ("gq", 1, "f"), ("gk", 1, "f"), ("gv", 2, "t"),
         ("gr", 2, "t"), ("bq", 2, "f"), ("bk", 2, "f"), ("bv", 2, "t"), ("ga", 2, "f"), ("gb", 2, "f"), ("wa", 2, "f"),
         ("wb", 2, "f"), ("wo2", 2, "t"), ("up", 8, "f"), ("dn", 8, "t"), ("pg", 2, "t")]
FIRST = {}
_n = 0
for _name, _c, _ in TILES:
    FIRST[_name] = _n
    _n += 1 if _name == "akv" else 2 * _c


def _order():
    o = []
    for name, k in ORDER:
        o += [(name, k, h) for h in range(1 if name in ("akv", "ple") else 2)]
    return o


ORDER = [("akv", 0), ("qk", 0), ("aq", 0), ("mv", 0), ("mo", 0), ("xk", 0), ("xk", 1), ("xv", 0), ("xv", 1), ("wo1",
         0), ("wo1", 1), ("xq", 0), ("xq", 1), ("xo", 0), ("xo", 1), ("pq", 0), ("pq", 1), ("pq", 2), ("pq", 3),
         ("gq", 0), ("gk", 0), ("gv", 0), ("gv", 1), ("gr", 0), ("gr", 1), ("bq", 0), ("bq", 1), ("bk", 0), ("bk",
         1), ("bv", 0), ("bv", 1), ("ga", 0), ("gb", 0), ("ga", 1), ("gb", 1), ("wa", 0), ("wa", 1), ("wb", 0),
         ("wb", 1), ("wo2", 0), ("wo2", 1), ("up", 0), ("up", 1), ("up", 2), ("up", 3), ("up", 4), ("up", 5), ("up",
         6), ("up", 7), ("dn", 0), ("dn", 1), ("dn", 2), ("dn", 3), ("dn", 4), ("dn", 5), ("dn", 6), ("dn", 7),
         ("ple", 0), ("pg", 0), ("pg", 1)]


class Tok:

    def __init__(self, q, sem=None, value=None):
        self.q, self.sem, self.value, self.used = q, sem, value, sem is not None


class Queue:

    def __init__(self, sem):
        self.sem, self.items = sem, []

    def __call__(self, fn, *waits):
        tok = Tok(self)
        self.items.append((fn, waits, tok))
        for w in waits:
            w.used = True
        return tok

    def dma(self, sem, fn, *waits):
        sem[1] += 16
        tok = Tok(self, sem[0], sem[1])
        self.items.append((fn, waits, tok))
        for w in waits:
            w.used = True
        return tok

    def number(self):
        n = 0
        for _, _, tok in self.items:
            if tok.used and tok.sem is None:
                n += 1
                tok.sem, tok.value = self.sem, n

    def emit(self, eng):
        seen = {}
        for fn, waits, tok in self.items:
            need = {}
            for w in waits:
                k = id(w.sem)
                if w.value > max(seen.get(k, 0), need.get(k, (0, None))[0]):
                    need[k] = (w.value, w.sem)
            for k, (v, s) in need.items():
                eng.wait_ge(s, v)
                seen[k] = v
            ins = fn(eng)
            if tok.sem is not None:
                ins.then_inc(tok.sem, 1 if tok.sem is self.sem else 16)


def program(nc, A, out, dbg=None):
    ctx = ExitStack()
    with ctx:
        def sb(name, shape, dt=F32):
            return ctx.enter_context(nc.sbuf_tensor(name, shape, dt))

        def sem(name):
            return ctx.enter_context(nc.semaphore(name))

        SP, ACTQ, V, PE, G = (Queue(sem(f"s_{n}")) for n in ("sp", "act", "dve", "pe", "pool"))
        S = ACTQ

        ring = sb("ring", [128, RING, 2048])
        rsem = [[sem(f"r{i}"), 0] for i in range(RING)]
        gsem = [[sem(f"g{i}"), 0] for i in range(6)]
        X = sb("X", [128, 2, 1024])
        XT = [sb(f"XT{z}", [128, 8, 256], F32R) for z in range(2)]
        HL = [[sb(f"hl{i}{z}", [128, 2048], F32R) for z in range(2)] for i in range(NHL)]
        with ExitStack() as plain:
            Bf = [plain.enter_context(nc.sbuf_tensor(f"B{i}", [128, 2048], F32)) for i in range(11)]
        Br = [sb(f"R{i}", [128, 2048], F32R) for i in range(11)]
        GB = sb("GB", [128, 1024])
        banks = [ctx.enter_context(nc.psum_tensor(f"ps{i}", [128, 512], F32)) for i in range(8)]
        ident = sb("ident", [128, 128])
        ones = sb("ones", [128, 128])
        M1 = sb("M1", [128, 256])
        DD = sb("DD", [128, 256])
        CT = sb("CT", [128, 128])
        sel = sb("sel", [4, 4, 128])
        scanm = sb("scanm", [128, 1024])
        cmask = sb("cmask", [128, 64])
        iot = sb("iot", [128, 16])
        ioi = sb("ioi", [128, 256], I32)
        gains = sb("gains", [128, 7, 8])
        small = sb("small", [128, 64])
        convw = sb("convw", [128, 4, 4])
        convb = sb("convb", [128, 4])
        sinkb = sb("sinkb", [128, 8])
        bif = sb("bif", [4, 2])
        thin = sb("thin", [128, 8, 24])
        thinr = [sb(f"thin{z}", [128, 8, 24], F32R) for z in range(2)]
        gw2 = sb("gw2", [16, 512])
        gb2 = sb("gb2", [128, 4])
        bqk = sb("bqk", [128, 2])
        skT = sb("skT", [128, 2, 128])
        diags = sb("diags", [128, 4, 128])
        st = sb("st", [128, 256])
        eidx = sb("eidx", [128, 2, 128], I32)
        gw = sb("gw", [128, 2, 128])
        av_ = sb("av_", [128, 2, 128])
        cf = sb("cf", [128, 2, 128])

        free = deque((i, ()) for i in range(8))

        def bank():
            i, toks = free.popleft()
            return i, banks[i], toks

        def put(i, *toks):
            free.append((i, toks))

        loaded, parted, slot_free, hl_free = [], [], {}, {}
        dma_order, used = [], [0]

        def load_half(n):
            name, k, hf = dma_order[n]
            i = n % RING
            src = A["wple"] if name == "ple" else A["wt"][FIRST[name] + 2 * k + hf]
            loaded.append(SP.dma(rsem[i], lambda e: e.dma_start(ring[:, i, :], src), *slot_free.get(n - RING, ())))

        def part_half(n):
            i, j = n % RING, n % NHL
            hi, lo = HL[j]
            fr = hl_free.get(n - NHL, ())
            a = S(lambda e: e.activation(hi[:, :], ring[:, i, :], ACT.Copy), loaded[n], *fr)
            b = V(lambda e: e.tensor_tensor(lo[:, :], ring[:, i, :], hi[:, :].bitcast(F32), ALU.subtract), a)
            slot_free[n] = (b,)
            parted.append(b)

        def half(name, k, hf):
            n = used[0]
            used[0] += 1
            if ORDER is None:
                dma_order.append((name, k, hf))
            assert dma_order[n] == (name, k, hf), (n, dma_order[n], name, k, hf)
            while len(parted) < min(n + NHL, len(dma_order)):
                while len(loaded) < min(len(parted) + RING, len(dma_order)):
                    load_half(len(loaded))
                part_half(len(parted))
            return HL[n % NHL], n, parted[n]

        if ORDER is not None:
            dma_order = _order()

        sconst = {}

        def cload(dst, src, name, q=SP):
            s = [sem(f"c_{name}"), 0]
            return q.dma(s, lambda e: e.dma_start(dst, src))

        D = {}

        def debug(name, ap, *toks):
            if dbg is not None and name in dbg:
                s = [sem(f"d_{name}"), 0]
                t = SP.dma(s, lambda e: e.dma_start(dbg[name], ap), *toks)
                SP(lambda e: e.nop(), t)

        t_x = cload(X[:, :, :], A["x"].rearrange("(a p) d -> p a d", p=128), "x")
        t_gains = cload(gains[:, :, :], A["gains"], "gains", S)
        g_id0 = G(lambda e: e.memset(ident[:, :], 0.0))
        g_id = G(lambda e: e.affine_select(out=ident[:, :], in_=ident[:, :], compare_op=ALU.not_equal, fill=1.0,
                                           base=0, pattern=[[-1, 128]], channel_multiplier=1), g_id0)
        g_sel0 = G(lambda e: e.memset(sel[:, :, :], 0.0))
        g_sel = G(lambda e: e.affine_select(out=sel[:, :, :], in_=sel[:, :, :], compare_op=ALU.not_equal, fill=1.0,
                                            base=0, pattern=[[-1, 4], [0, 128]], channel_multiplier=1), g_sel0)
        g_m0 = G(lambda e: e.memset(M1[:, :], 0.0))
        g_m1a = G(lambda e: e.affine_select(out=M1[:, 0:128], in_=M1[:, 0:128], compare_op=ALU.is_gt, fill=NEG,
                                            base=0, pattern=[[1, 128]], channel_multiplier=-1), g_m0)
        g_m1 = G(lambda e: e.affine_select(out=M1[:, 128:256], in_=M1[:, 128:256], compare_op=ALU.is_ge, fill=NEG,
                                           base=0, pattern=[[-1, 128]], channel_multiplier=1), g_m0)
        g_ct0 = G(lambda e: e.memset(CT[:, :], 0.0))
        g_ct = G(lambda e: e.affine_select(out=CT[:, :], in_=CT[:, :], compare_op=ALU.is_ge, fill=-NEG,
                                           base=0, pattern=[[1, 128]], channel_multiplier=-1), g_ct0)
        epsc = sb("epsc", [128, 1])
        g_eps = G(lambda e: e.memset(epsc[:, :], EPS))
        g_on = G(lambda e: e.memset(ones[:, :], 1.0))
        g_io = G(lambda e: e.iota(ioi[:, :], pattern=[[1, 256]], base=-128, channel_multiplier=-1))
        g_dd0 = G(lambda e: e.tensor_copy(DD[:, :], ioi[:, :]), g_io)
        g_dd = G(lambda e: e.affine_select(out=DD[:, :], in_=DD[:, :], compare_op=ALU.is_ge, fill=NEG,
                                           base=128, pattern=[[-1, 256]], channel_multiplier=1), g_dd0)
        g_i16a = G(lambda e: e.iota(ioi[:, 0:16], pattern=[[1, 16]], base=0, channel_multiplier=0), g_dd0)
        g_i16 = G(lambda e: e.tensor_copy(iot[:, :], ioi[:, 0:16]), g_i16a)
        g_s0 = G(lambda e: e.memset(scanm[:, :], 1.0))
        g_scan = G(lambda e: e.memset(scanm[:, :].rearrange("p (a b) -> p a b", b=64)[:, :, 0:1], 0.0), g_s0)
        g_c0 = G(lambda e: e.memset(cmask[:, :], 1.0))
        for b in range(2):
            g_cm = G(lambda e, b=b: e.affine_select(out=cmask[64 * b:64 * b + 64, :], in_=cmask[64 * b:64 * b + 64, :],
                                                    compare_op=ALU.is_ge, fill=0.0, base=0, pattern=[[1, 64]],
                                                    channel_multiplier=-1), g_c0)
        g_last = G(lambda e: e.memset(small[:, 60:61], 0.0), g_id, g_sel, g_m1a, g_m1, g_ct, g_on, g_dd, g_i16, g_scan, g_cm)
        t_mem = cload(Bf[0][:, :].rearrange("p (a d) -> p a d", a=2),
                      A["mem"].rearrange("(a p) d -> p a d", p=128), "mem", S)
        t_cw = cload(convw[:, :, :], A["convw"], "convw", S)
        t_cb = cload(convb[:, :], A["convb"], "convb", S)
        t_bif = cload(bif[:, :], A["bif"], "bif", S)
        t_sink = cload(sinkb[:, :], A["sinks"].partition_broadcast(128), "sinks", S)
        t_gm = cload(GB[:, 0:512], A["gmh"].partition_broadcast(128), "gmh", S)
        t_sk = cload(skT[:, :, :], A["sk"], "sk", S)
        t_thin = cload(thin[:, :, :], A["thin"], "thin", S)
        t_gw2 = cload(gw2[:, :], A["gw2"], "gw2", S)
        t_gb2 = cload(gb2[:, :], A["gb2"], "gb2", S)
        t_bqk = cload(bqk[:, :], A["bqk"], "bqk", S)

        dturn = [0]
        dfree = [(), (), (), ()]
        stat = [0]

        def col(n=1):
            if stat[0] + n > 256:
                stat[0] = 0
            c = stat[0]
            stat[0] += n
            return st[:, c:c + n]

        def rstd(ss, n, *toks):
            w = ss.shape[1]
            v, q = col(w), col(w)
            a = V(lambda e: e.tensor_scalar(v, ss, 1.0 / n, EPS, ALU.mult, ALU.add), *toks)
            b = S(lambda e: e.activation(ss, v, ACT.Sqrt), a)
            b = V(lambda e: e.reciprocal(ss, ss), b)
            a = V(lambda e: e.tensor_tensor(q, v, ss, ALU.mult), b)
            a = V(lambda e: e.tensor_tensor(q, q, ss, ALU.mult), a)
            a = V(lambda e: e.tensor_scalar(q, q, -0.5, 1.5, ALU.mult, ALU.add), a)
            return V(lambda e: e.tensor_tensor(ss, ss, q, ALU.mult), a)

        def norm_cols(src, junk, tsrc, tjunk):
            r = []
            for tb in range(2):
                c = col()
                if tb == 0:
                    a = S(lambda e, c=c, tb=tb: e.activation(junk[:, tb, :], src[:, tb, :], ACT.Square, accum_out=c),
                          *tsrc, *tjunk)
                else:
                    a = V(lambda e, c=c, tb=tb: e.tensor_tensor_reduce(junk[:, tb, :], src[:, tb, :], src[:, tb, :],
                                                                       1.0, 0.0, ALU.mult, ALU.add, c), *tsrc, *tjunk)
                r.append((c, rstd(c, 1024, a)))
            return r

        def transposed(src, cols, gain, dst, tsrc, tdst):
            dg = []
            for tb in range(2):
                j = dturn[0] % 4
                dturn[0] += 1
                if cols is None:
                    dg.append((ident[:, :], g_id, None))
                    continue
                c, tc = cols[tb]
                t = V(lambda e, j=j, c=c: e.tensor_scalar(diags[:, j, :], ident[:, :], c, None, ALU.mult), tc, g_id,
                      *dfree[j])
                dg.append((diags[:, j, :], t, j))
            res = []
            for k in range(0, 8, 2):
                i, ps, tf = bank()
                for tb in range(2):
                    for kk in range(2):
                        m = PE(lambda e, k=k, kk=kk, tb=tb, ps=ps: e.matmul(
                            ps[:, kk * 256 + tb * 128:kk * 256 + tb * 128 + 128],
                            src[:, tb, (k + kk) * 128:(k + kk + 1) * 128], dg[tb][0], start=True, stop=True),
                            *tf, *tsrc, dg[tb][1])
                if gain is None:
                    t = parts(dst, slice(k, k + 2), ps[:, :].rearrange("p (a b) -> p a b", a=2), m, *tdst)
                else:
                    for kk in range(2):
                        a = S(lambda e, k=k + kk, p_=ps[:, kk * 256:kk * 256 + 256]: e.activation(
                            dst[0][:, k, :], p_, ACT.Copy, scale=gain[:, k:k + 1]), m, *tdst, t_gains)
                    for kk in range(2):
                        t = V(lambda e, k=k + kk, p_=ps[:, kk * 256:kk * 256 + 256]: e.scalar_tensor_tensor(
                            dst[1][:, k, :], p_, gain[:, k:k + 1], dst[0][:, k, :].bitcast(F32), ALU.mult,
                            ALU.subtract), m, a, *tdst, t_gains)
                put(i, t)
                res.append(t)
            for _, _, j in dg:
                if j is not None:
                    dfree[j] = (m,)
            return res

        def parts(dst, c, src, *toks):
            a = S(lambda e: e.activation(dst[0][:, c, :], src, ACT.Copy), *toks)
            return V(lambda e: e.tensor_tensor(dst[1][:, c, :], src, dst[0][:, c, :].bitcast(F32), ALU.subtract),
                     a, *toks)

        TERMS = [(0, 0), (0, 1), (1, 0)]

        def prod(ps, lhs, rhs, ks, start=True, stop=True, *toks):
            ks = list(ks)
            for a, b in TERMS:
                for k in ks:
                    m = PE(lambda e, a=a, b=b, k=k, x=lhs(a, k), y=rhs(b, k): e.matmul(
                        ps, x, y, start=start and (a, b, k) == (0, 0, ks[0]),
                        stop=stop and (a, b, k) == (1, 0, ks[-1])), *toks)
            return m

        def layer_fm(name, k, src, tsrc, evac, res=None):
            for hf in range(2):
                w, n, tw = half(name, k, hf)
                w = [p[:, :].rearrange("p (k n) -> p k n", k=8) for p in w]
                b, ps, tf = bank()
                for c in range(2):
                    m = prod(ps[:, c * 256:c * 256 + 256], lambda a, k, c=c: w[a][:, k, c * 128:c * 128 + 128],
                             lambda b_, k: src[b_][:, k, :], range(8), True, True, tw, *tsrc, *tf)
                hl_free[n] = (m,)
                t = evac(hf, ps[:, :].rearrange("p (a b) -> p a b", a=2), m)
                put(b, t)
                if res is not None:
                    res.append(t)
                yield

        def layer_tm(name, k, src, tsrc, evac, res=None, bk=None, start=True, stop=True):
            own = bk is None
            bk = [bank() for _ in range(2)] if own else bk
            for hf in range(2):
                w, n, tw = half(name, k, hf)
                w = [p[:, :].rearrange("p (k n) -> p k n", k=4) for p in w]
                for tb in range(2):
                    m = prod(bk[tb][1][:, :], lambda a, k, tb=tb, hf=hf: src[a][:, 4 * hf + k, tb * 128:tb * 128 + 128],
                             lambda b_, k: w[b_][:, k, :], range(4), start and hf == 0, stop and hf == 1,
                             tw, *tsrc, *bk[tb][2])
                    if hf == 1 and stop:
                        t = evac(tb, bk[tb][1], m)
                        put(bk[tb][0], t)
                        if res is not None:
                            res.append(t)
                hl_free[n] = (m,)
                yield

        def run(*gens):
            for g in gens:
                for _ in g:
                    pass

        fills = deque()

        def fill(n=1):
            while n and fills:
                if callable(fills[0]):
                    fills[0] = fills[0]()
                if next(fills[0], fills) is fills:
                    fills.popleft()
                else:
                    n -= 1

        junk = Bf[9][:, :].rearrange("p (a d) -> p a d", a=2)
        cols_x = norm_cols(X, junk, [t_x], [])
        t_xt = transposed(X, cols_x, gains[:, 0, :], XT, [t_x], [])

        t_th = S(lambda e: e.activation(thinr[0][:, :, :], thin[:, :, :], ACT.Copy), t_thin)
        t_th = V(lambda e: e.tensor_tensor(thinr[1][:, :, :], thin[:, :, :], thinr[0][:, :, :].bitcast(F32),
                                           ALU.subtract), t_th)
        bG, psG, tf = bank()
        for z in range(2):
            mg = prod(psG[0:4, z * 256:z * 256 + 256], lambda a, k, z=z: thinr[a][:, k, 4 * z:4 * z + 4],
                      lambda b_, k: XT[b_][:, k, :], range(8), True, True, t_th, *t_xt, *tf)
        gt = Bf[4][0:4, 0:2048].rearrange("p (a b) -> p a b", b=256)
        ip, z_, ab, lf, bb, aa, MM, mm_ = (gt[:, j, :] for j in range(8))
        v1 = V(lambda e: e.tensor_scalar(ip, psG[0:4, 0:256], bif[:, 0:1], None, ALU.add), mg, t_bif)
        v2 = V(lambda e: e.tensor_scalar(z_, psG[0:4, 256:512], bif[:, 1:2], None, ALU.add), mg, t_bif)
        put(bG, v2)
        v3 = S(lambda e: e.activation(ab, z_, ACT.Abs), v2)
        a1 = S(lambda e: e.activation(ab, ab, ACT.Exp, scale=-1.0), v3)
        a2 = S(lambda e: e.activation(ab, ab, ACT.Ln, bias=1.0), a1)
        v4 = V(lambda e: e.scalar_tensor_tensor(lf, z_, 0.0, ab, ALU.min, ALU.subtract), a2)
        g_o4 = V(lambda e: e.memset(mm_, 1.0))
        v5 = V(lambda e: e.tensor_tensor_scan(bb, mm_, lf, 0.0, ALU.mult, ALU.add), v4, g_o4)
        v6 = V(lambda e: e.tensor_tensor(aa, ip, bb, ALU.subtract), v5, v1)
        v6b = V(lambda e: e.memset(z_, 0.0), v4)
        v7 = V(lambda e: e.tensor_tensor_scan(MM, z_, aa, 0.0, ALU.add, ALU.max), v6, v6b)
        v8 = V(lambda e: e.tensor_tensor(mm_, bb, MM, ALU.add), v7)
        akT = Bf[3][:, 1024:1280]
        avt = Bf[3][:, 1280:1536].rearrange("p (a d) -> p a d", a=2)
        bK, psK, tf = bank()
        wk, n_, tw = half("akv", 0, 0)
        wk = [p[:, :].rearrange("p (k n) -> p k n", k=8) for p in wk]
        prod(psK[:, 0:256], lambda a, k: wk[a][:, k, 0:128], lambda b_, k: XT[b_][:, k, :], range(8), True, True,
             tw, *t_xt, *tf)
        for tb in range(2):
            m2 = prod(psK[:, 256 + tb * 128:384 + tb * 128],
                      lambda a, k, tb=tb: XT[a][:, k, tb * 128:tb * 128 + 128],
                      lambda b_, k: wk[b_][:, k, 128:256], range(8), True, True, tw, *t_xt, *tf)
        hl_free[n_] = (m2,)
        t_ak = S(lambda e: e.activation(akT, psK[:, 0:256], ACT.Copy), m2)
        t_av = S(lambda e: e.activation(avt, psK[:, 256:512].rearrange("p (a d) -> p a d", a=2), ACT.Copy), m2)
        put(bK, t_av)

        qkT = Bf[2][:, 0:1024].rearrange("p (a t) -> p a t", a=4)
        yv = Bf[2][:, 1024:2048].rearrange("p (a t) -> p a t", a=4)
        t_qk = []

        def ev_conv(hf, ps, m):
            for c in range(2):
                ch = 2 * hf + c
                t = V(lambda e, ch=ch, c=c: e.tensor_scalar(yv[:, ch, :], ps[:, c, :], convw[:, ch, 3:4],
                                                            convb[:, ch:ch + 1], ALU.mult, ALU.add), m, t_cw, t_cb)
                for s in range(1, 4):
                    t = V(lambda e, ch=ch, c=c, s=s: e.scalar_tensor_tensor(
                        yv[:, ch, s:256], ps[:, c, 0:256 - s], convw[:, ch, 3 - s:4 - s], yv[:, ch, s:256],
                        ALU.mult, ALU.add), t)
                t_qk.append(S(lambda e, ch=ch: e.activation(qkT[:, ch, :], yv[:, ch, :], ACT.Silu), t))
            return t

        run(layer_fm("qk", 0, XT, t_xt, ev_conv))
        debug("qkT", qkT, *t_qk)

        aqT = Bf[3][:, 0:1024].rearrange("p (a t) -> p a t", a=4)
        t_aq = []
        run(layer_fm("aq", 0, XT, t_xt, lambda hf, ps, m: S(
            lambda e: e.activation(aqT[:, 2 * hf:2 * hf + 2, :], ps, ACT.Copy), m), t_aq))

        V1 = Bf[7][:, 0:1032].rearrange("p (a h d) -> p a h d", a=2, h=4)
        t_v1o = V(lambda e: e.memset(V1[:, :, :, 128:129], 1.0))
        t_mv = []
        run(layer_tm("mv", 0, XT, t_xt, lambda tb, ps, m: S(
            lambda e: e.activation(V1[:, tb, :, 0:128], ps[:, :].rearrange("p (h d) -> p h d", h=4), ACT.Copy), m),
            t_mv))
        og = Bf[5][:, 0:1024].rearrange("p (a d) -> p a d", a=2)

        def ev_mo(tb, ps, m):
            t = S(lambda e: e.activation(og[:, tb, :], ps[:, :], ACT.Sigmoid), m)
            D[f"og{tb}"] = V(lambda e: e.tensor_tensor(og[:, tb, :], og[:, tb, :], GB[:, 0:512], ALU.mult), t, t_gm)
            return t

        run(layer_tm("mo", 0, XT, t_xt, ev_mo))
        t_og = [D["og0"], D["og1"]]

        bA, psA, tf = bank()
        for tb in range(2):
            for z, src in enumerate((aa, mm_)):
                mt = PE(lambda e, tb=tb, z=z, src=src: e.transpose(psA[:, 8 * tb + 4 * z:8 * tb + 4 * z + 4],
                                                                   src[:, tb * 128:tb * 128 + 128], ident[0:4, 0:4]),
                        v8, g_id, *tf)
        ac = small[:, 0:8].rearrange("p (a h) -> p a h", a=2)
        em = small[:, 8:16].rearrange("p (a h) -> p a h", a=2)
        p4 = psA[:, 0:16].rearrange("p (a z h) -> p a z h", a=2, z=2)
        t_ac = S(lambda e: e.activation(ac, p4[:, :, 0, :], ACT.Copy), mt)
        t_em = S(lambda e: e.activation(em, p4[:, :, 1, :], ACT.Exp, scale=-1.0), mt)
        put(bA, t_em)

        memT = [Br[j][:, :].rearrange("p (k t) -> p k t", k=8) for j in (1, 10)]
        mem = Bf[0][:, :].rearrange("p (a d) -> p a d", a=2)
        cols_m = norm_cols(mem, junk, [t_mem], t_xt)
        KT = Bf[8][:, :].rearrange("p (k t) -> p k t", k=8)
        VX = Bf[6][:, :].rearrange("p (a d) -> p a d", a=2)
        t_mT, t_kx, t_vx = [], [], []

        def mem_transposed():
            t_mT.extend(transposed(mem, cols_m, gains[:, 1, :], memT, [t_mem], []))
            yield

        fills.append(mem_transposed)
        for k in range(2):
            fills.append(lambda k=k: layer_fm("xk", k, memT, t_mT, lambda hf, ps, m: S(
                lambda e: e.activation(KT[:, 4 * k + 2 * hf:4 * k + 2 * hf + 2, :], ps, ACT.Copy), m), t_kx))
        for k in range(2):
            fills.append(lambda k=k: layer_tm("xv", k, memT, t_mT, lambda tb, ps, m: S(
                lambda e: e.activation(VX[:, tb, k * 512:k * 512 + 512], ps[:, :], ACT.Copy), m), t_vx))
        hm = Bf[5][:, 1024:2048].rearrange("p (a d) -> p a d", a=2)
        dbuf = [Bf[9][:, 0:384], Bf[9][:, 384:768]]
        gbuf = [Bf[9][:, 768:1152], Bf[9][:, 1152:1536]]
        gfree = [tuple(cols_m[j][1] for j in range(2))] * 2
        Gt = {}
        ssh = col(8)
        t_h = []
        for h in range(5):
            if h < 4:
                po = 64 * (h % 2)
                qh, kh = qkT[po:po + 64, h // 2, :], qkT[po:po + 64, 2 + h // 2, :]
                bM, psM, tf = bank()
                mM = PE(lambda e, h=h, psM=psM: e.matmul(psM[:, 0:256], sel[:, h, :], MM, start=True, stop=True),
                        v8, g_sel, *tf)
                d, g = dbuf[h % 2], gbuf[h % 2]
                fr = gfree[h % 2]
                e1 = V(lambda e, d=d, psM=psM: e.tensor_tensor(d[:, 0:128], psM[:, 0:128], CT[:, :], ALU.add),
                       mM, g_ct, *fr)
                e2 = V(lambda e, d=d, psM=psM: e.tensor_tensor(d[:, 256:384], psM[:, 128:256], CT[:, :], ALU.add),
                       mM, g_ct, *fr)
                e3 = V(lambda e, d=d, psM=psM: e.tensor_copy(d[:, 128:256], psM[:, 128:256]), mM, *fr)
                put(bM, e3)
                x1 = S(lambda e, d=d, h=h: e.activation(d[:, 0:256], d[:, 0:256], ACT.Exp, scale=-1.0,
                                                        bias=ac[:, 0, h:h + 1]), e3, t_ac)
                x2 = S(lambda e, d=d, h=h: e.activation(d[:, 256:384], d[:, 256:384], ACT.Exp, scale=-1.0,
                                                        bias=ac[:, 1, h:h + 1]), e3, t_ac)
                bS, psS, tf = bank()
                PE(lambda e, psS=psS, kh=kh, qh=qh: e.matmul(psS[:, 0:256], kh[:, 0:128], qh, start=True, stop=True),
                   *t_qk, *tf)
                mS = PE(lambda e, psS=psS, kh=kh, qh=qh: e.matmul(psS[:, 256:384], kh[:, 128:256], qh[:, 128:256],
                                                                  start=True, stop=True), *t_qk, *tf)
                tg = V(lambda e, g=g, psS=psS, d=d: e.scalar_tensor_tensor(g, psS[:, 0:384], 0.125, d, ALU.mult,
                                                                           ALU.mult), mS, x1, x2, *fr)
                put(bS, tg)
                Gt[h] = (g, tg)
                fill()
            if h >= 1:
                p = h - 1
                g, tg = Gt[p]
                bO, psO, tf = bank()
                PE(lambda e, g=g, p=p, psO=psO: e.matmul(psO[:, 0:129], g[:, 0:128], V1[:, 0, p, :], start=True,
                                                         stop=True), tg, *t_mv, t_v1o, *tf)
                PE(lambda e, g=g, p=p, psO=psO: e.matmul(psO[:, 129:258], g[:, 128:256], V1[:, 0, p, :], start=True,
                                                         stop=False), tg)
                mO = PE(lambda e, g=g, p=p, psO=psO: e.matmul(psO[:, 129:258], g[:, 256:384], V1[:, 1, p, :],
                                                              start=False, stop=True), tg)
                gfree[p % 2] = (mO,)
                dn = col(2)
                n1 = S(lambda e, dn=dn, psO=psO: e.activation(
                    dn, psO[:, 0:258].rearrange("p (a d) -> p a d", a=2)[:, :, 128], ACT.Abs), mO)
                n2 = V(lambda e, dn=dn, p=p: e.tensor_tensor(dn, dn, em[:, :, p], ALU.max), n1, t_em)
                n3 = V(lambda e, dn=dn: e.reciprocal(dn, dn), n2)
                for tb in range(2):
                    n4 = V(lambda e, dn=dn, tb=tb, p=p, psO=psO: e.tensor_scalar(
                        hm[:, tb, p * 128:p * 128 + 128], psO[:, tb * 129:tb * 129 + 128], dn[:, tb:tb + 1], None,
                        ALU.mult), n3)
                    t_h.append(S(lambda e, tb=tb, p=p: e.activation(
                        Bf[9][:, 1536 + tb * 128:1664 + tb * 128], hm[:, tb, p * 128:p * 128 + 128], ACT.Square,
                        accum_out=ssh[:, tb * 4 + p:tb * 4 + p + 1]), n4, *t_h[-1:]))
                put(bO, n4)
        trs = rstd(ssh, 128, *t_h)
        for tb in range(2):
            for p in range(4):
                tn = V(lambda e, tb=tb, p=p: e.scalar_tensor_tensor(
                    hm[:, tb, p * 128:p * 128 + 128], hm[:, tb, p * 128:p * 128 + 128],
                    ssh[:, tb * 4 + p:tb * 4 + p + 1], og[:, tb, p * 128:p * 128 + 128], ALU.mult, ALU.mult),
                    trs, *t_og)
        debug("hm", hm, tn)
        t_gffn = S.dma([sem("c_gffn"), 0], lambda e: e.dma_start(GB[:, :], A["gffn"].partition_broadcast(128)), *t_og)

        mixT = [Br[j][:, :].rearrange("p (k t) -> p k t", k=8) for j in (0, 4)]

        attP = [Bf[9][:, 0:384], Bf[9][:, 384:768]]
        attT = [Bf[9][:, 768:1152], Bf[9][:, 1152:1536]]
        pfree, tfree = [gfree[0]] * 2, [gfree[0] + gfree[1]] * 2
        pfree = [gfree[0] + gfree[1]] * 2
        info = {}
        t_mix = []
        for h in range(10):
            if h < 8:
                po = 64 * (h // 4)
                qh, kh = aqT[po:po + 64, h % 4, :], akT[po:po + 64, :]
                bS, psS, tf = bank()
                PE(lambda e, psS=psS, kh=kh, qh=qh: e.matmul(psS[:, 0:128], qh[:, 0:128], kh[:, 0:128], start=True,
                                                             stop=True), *t_aq, t_ak, *tf)
                mS = PE(lambda e, psS=psS, kh=kh, qh=qh: e.matmul(psS[:, 128:384], qh[:, 128:256], kh, start=True,
                                                                  stop=True), *t_aq, t_ak, *tf)
                P = attP[h % 2]
                mx = col(2)
                sm = col(2)
                V(lambda e, P=P, psS=psS, mx=mx: e.tensor_tensor_reduce(P[:, 0:128], psS[:, 0:128], M1[:, 128:256],
                                                                        0.125, NEG, ALU.add, ALU.max, mx[:, 0:1]),
                  mS, g_m1, g_m1a, *pfree[h % 2])
                r2 = V(lambda e, P=P, psS=psS, mx=mx: e.tensor_tensor_reduce(P[:, 128:384], psS[:, 128:384], M1[:, :],
                                                                             0.125, NEG, ALU.add, ALU.max, mx[:, 1:2]),
                       mS, g_m1, g_m1a, *pfree[h % 2])
                put(bS, r2)
                r3 = V(lambda e, mx=mx, h=h: e.tensor_scalar(mx, mx, sinkb[:, h:h + 1], -1.0, ALU.max, ALU.mult), r2,
                       t_sink)
                for tb, (c0, c1) in enumerate(((0, 128), (128, 384))):
                    x1 = S(lambda e, P=P, c0=c0, c1=c1, tb=tb, mx=mx, sm=sm: e.activation(
                        P[:, c0:c1], P[:, c0:c1], ACT.Exp, bias=mx[:, tb:tb + 1], accum_out=sm[:, tb:tb + 1]), r3)
                es = col(2)
                x3 = S(lambda e, es=es, mx=mx, h=h: e.activation(es, mx, ACT.Exp, bias=sinkb[:, h:h + 1]), r3)
                r4 = V(lambda e, sm=sm, es=es: e.tensor_tensor(sm, sm, es, ALU.add), x1, x3)
                r5 = V(lambda e, sm=sm: e.reciprocal(sm, sm), r4)
                V(lambda e, P=P, sm=sm: e.tensor_scalar(P[:, 0:128], P[:, 0:128], sm[:, 0:1], None, ALU.mult), r5)
                r6 = V(lambda e, P=P, sm=sm: e.tensor_scalar(P[:, 128:384], P[:, 128:384], sm[:, 1:2], None, ALU.mult),
                       r5)
                info[h] = (P, r6)
                fill()
            if 1 <= h < 9:
                p = h - 1
                P, tP = info[p]
                bT, psT, tf = bank()
                for j in range(3):
                    mT = PE(lambda e, j=j, P=P, psT=psT: e.transpose(psT[:, j * 128:j * 128 + 128],
                                                                     P[:, j * 128:j * 128 + 128], ident[:, :]),
                            tP, g_id, *tf)
                PT = attT[p % 2]
                t = S(lambda e, PT=PT, psT=psT: e.activation(PT, psT[:, 0:384], ACT.Copy), mT, *tfree[p % 2])
                put(bT, t)
                pfree[p % 2] = (mT,)
                info[p] = (PT, t)
            if h >= 2:
                p = h - 2
                PT, tP = info[p]
                kv = p // 4
                if p % 2 == 0:
                    bV, psV, tfV = bank()
                po = 64 * (p % 2)
                vs = [avt[:, s, kv * 64:kv * 64 + 64] for s in range(2)]
                PE(lambda e, PT=PT, vs=vs, po=po, psV=psV: e.matmul(psV[po:po + 64, 0:128], vs[0], PT[:, 0:128],
                                                                    start=True, stop=True), tP, t_av, *tfV)
                PE(lambda e, PT=PT, vs=vs, po=po, psV=psV: e.matmul(psV[po:po + 64, 128:256], vs[0], PT[:, 128:256],
                                                                    start=True, stop=False), tP)
                mV = PE(lambda e, PT=PT, vs=vs, po=po, psV=psV: e.matmul(psV[po:po + 64, 128:256], vs[1],
                                                                         PT[:, 256:384], start=False, stop=True), tP)
                tfree[p % 2] = (mV,)
                if p % 2 == 1:
                    t = parts(mixT, slice(4 + p // 2, 5 + p // 2), psV[:, 0:256].unsqueeze(1), mV, *t_mT, mM)
                    put(bV, t)
                    t_mix.append(t)
        fill(99)
        for c in range(0, 4, 2):
            b, ps, tf = bank()
            for cc in range(2):
                for tb in range(2):
                    m = PE(lambda e, c=c, cc=cc, tb=tb, ps=ps: e.transpose(
                        ps[:, cc * 256 + tb * 128:cc * 256 + tb * 128 + 128],
                        hm[:, tb, (c + cc) * 128:(c + cc + 1) * 128], ident[:, :]), tn, g_id, *tf)
            t = parts(mixT, slice(c, c + 2), ps[:, :].rearrange("p (a b) -> p a b", a=2), m, *t_mT, mM)
            put(b, t)
            t_mix.append(t)
        tX = [t_x]

        def ev_res(k, tx, res):
            def ev(tb, ps, m):
                t = V(lambda e: e.tensor_tensor(X[:, tb, k * 512:k * 512 + 512], ps[:, :],
                                                X[:, tb, k * 512:k * 512 + 512], ALU.add), m, *tx)
                res.append(t)
                return t
            return ev

        t_h1 = []
        for k in range(2):
            run(layer_tm("wo1", k, mixT, t_mix, ev_res(k, t_xt, t_h1)))
        debug("h1", X[:, :, :], *t_h1)

        cols_h = norm_cols(X, junk, t_h1, [mV])
        t_xt = transposed(X, cols_h, gains[:, 2, :], XT, t_h1, [])
        QT = Bf[2][:, :].rearrange("p (k t) -> p k t", k=8)
        t_qx = []
        for k in range(2):
            run(layer_fm("xq", k, XT, t_xt, lambda hf, ps, m, k=k: S(
                lambda e: e.activation(QT[:, 4 * k + 2 * hf:4 * k + 2 * hf + 2, :], ps, ACT.Copy), m), t_qx))
        oT = [Br[j][:, :].rearrange("p (k t) -> p k t", k=8) for j in (3, 7)]
        attP = [Bf[9][:, 0:512], Bf[9][:, 512:1024]]
        attT = [Bf[9][:, 1024:1536], Bf[9][:, 1536:2048]]
        pfree = [t_xt, t_xt]
        tfree = [t_xt, t_xt]
        t_o = []
        for h in range(6):
            if h < 4:
                b, ps, tf = bank()
                for tb in range(2):
                    for kk in range(2):
                        m = PE(lambda e, h=h, tb=tb, kk=kk, ps=ps: e.matmul(
                            ps[:, tb * 256:tb * 256 + 256], QT[:, 2 * h + kk, tb * 128:tb * 128 + 128],
                            KT[:, 2 * h + kk, :], start=(kk == 0), stop=(kk == 1)), *t_qx, *t_kx, *tf)
                P = attP[h % 2]
                mx, sm = col(2), col(2)
                r1 = V(lambda e, mx=mx, ps=ps: e.tensor_reduce(mx, ps[:, :].rearrange("p (a b) -> p a b", a=2), AX,
                                                               ALU.max), m)
                r2 = V(lambda e, mx=mx: e.tensor_scalar(mx, mx, -0.0625, None, ALU.mult), r1)
                for tb in range(2):
                    x = S(lambda e, tb=tb, P=P, ps=ps, mx=mx, sm=sm: e.activation(
                        P[:, tb * 256:tb * 256 + 256], ps[:, tb * 256:tb * 256 + 256], ACT.Exp, scale=0.0625,
                        bias=mx[:, tb:tb + 1], accum_out=sm[:, tb:tb + 1]), r2, *pfree[h % 2])
                put(b, x)
                r3 = V(lambda e, sm=sm: e.reciprocal(sm, sm), x)
                for tb in range(2):
                    r4 = V(lambda e, tb=tb, P=P, sm=sm: e.tensor_scalar(
                        P[:, tb * 256:tb * 256 + 256], P[:, tb * 256:tb * 256 + 256], sm[:, tb:tb + 1], None,
                        ALU.mult), r3)
                info[h] = (P, r4)
            if 1 <= h < 5:
                p = h - 1
                P, tP = info[p]
                b, ps, tf = bank()
                for mb in range(2):
                    for tb in range(2):
                        m = PE(lambda e, mb=mb, tb=tb, P=P, ps=ps: e.transpose(
                            ps[:, mb * 256 + tb * 128:mb * 256 + tb * 128 + 128],
                            P[:, tb * 256 + mb * 128:tb * 256 + mb * 128 + 128], ident[:, :]), tP, *tf)
                PT = attT[p % 2]
                t = V(lambda e, PT=PT, ps=ps: e.tensor_copy(PT, ps[:, :]), m, *tfree[p % 2])
                put(b, t)
                pfree[p % 2] = (m,)
                info[p] = (PT, t)
            if h >= 2:
                p = h - 2
                PT, tP = info[p]
                b, ps, tf = bank()
                for dc in range(2):
                    for mb in range(2):
                        m = PE(lambda e, p=p, dc=dc, mb=mb, PT=PT, ps=ps: e.matmul(
                            ps[:, dc * 256:dc * 256 + 256], VX[:, mb, p * 256 + dc * 128:p * 256 + dc * 128 + 128],
                            PT[:, mb * 256:mb * 256 + 256], start=(mb == 0), stop=(mb == 1)), tP, *t_vx, *tf)
                tfree[p % 2] = (m,)
                t = parts(oT, slice(2 * p, 2 * p + 2), ps[:, :].rearrange("p (a b) -> p a b", a=2), m)
                put(b, t)
                t_o.append(t)
        mx_last = m
        t_h2 = []
        for k in range(2):
            run(layer_tm("xo", k, oT, t_o, ev_res(k, [], t_h2)))
        debug("h2", X[:, :, :], *t_h2)

        cols_h = norm_cols(X, junk, t_h2, [mx_last])
        t_xt = transposed(X, cols_h, gains[:, 3, :], XT, t_h2, [])
        XG = Bf[0][:, :].rearrange("p (a d) -> p a d", a=2)
        t_xg, t_gfin = [], []
        acc = []
        for tb in range(2):
            for hf in range(2):
                acc.append(bank())
        qhT = Bf[1][:, 0:512].rearrange("p (c t) -> p c t", c=2)
        sc = [Bf[2][:, 512 * j:512 * j + 512].rearrange("p (a c n) -> p a c n", a=2, c=2) for j in range(2)]
        sc2 = Bf[2][:, 1024:1280].rearrange("p (c n) -> p c n", c=2)
        vt = Bf[3][:, 0:32].rearrange("p (c n) -> p c n", c=2)
        it = sb("it", [128, 2, 16], U32)
        itf = Bf[3][:, 64:96].rearrange("p (c n) -> p c n", c=2)
        cand = Bf[4][:, 0:256]
        cand2 = Bf[4][:, 512:768]
        ts = Bf[3][:, 128:144]
        pos = sb("pos", [128, 16], U32)
        pi = sb("pi", [128, 2, 16], U32)
        pf = Bf[3][:, 160:192].rearrange("p (c n) -> p c n", c=2)
        eq = [Bf[5][:, j * 256:j * 256 + 256].rearrange("p (k n) -> p k n", n=16) for j in range(2)]
        si = Bf[3][:, 224:256].rearrange("p (c n) -> p c n", c=2)
        ei = Bf[3][:, 288:304]
        smx = Bf[3][:, 320:322]
        t_idx, t_gw, t_sc = {}, {}, {}
        qh_free, chain = [list(t_h1)], [t_h2[-1]]
        sc_free = [list(t_h2), list(t_h2)]

        def top16(src, work, vals, idx, *toks):
            a = V(lambda e: e.max(out=vals[:, 0:8], in_=src), *toks)
            yield
            V(lambda e: e.max_index(out=idx[:, 0:8], in_max=vals[:, 0:8], in_values=src), a)
            yield
            c = V(lambda e: e.match_replace(out=work, in_to_replace=vals[:, 0:8], in_values=src, imm_value=-3.0e38), a)
            yield
            d = V(lambda e: e.max(out=vals[:, 8:16], in_=work), c)
            yield
            chain[0] = V(lambda e: e.max_index(out=idx[:, 8:16], in_max=vals[:, 8:16], in_values=work), d)
            yield

        def peer_query(h):
            w, n, tw = half("pq", h // 2, h % 2)
            w = [p[:, :].rearrange("p (k n) -> p k n", k=8) for p in w]
            b, ps, tf = bank()
            for c in range(2):
                m = prod(ps[:, c * 256:c * 256 + 256], lambda a, k, c=c: w[a][:, k, c * 128:c * 128 + 128],
                         lambda b_, k: XT[b_][:, k, :], range(8), True, True, tw, *t_xt, *tf)
            hl_free[n] = (m,)
            tq = S(lambda e: e.activation(qhT, ps[:, :].rearrange("p (a b) -> p a b", a=2), ACT.Copy), m, *qh_free[0])
            put(b, tq)
            return tq

        def peer_scores(h, tq):
            b, ps, tf = bank()
            for tb in range(2):
                for c in range(2):
                    m = PE(lambda e, c=c, tb=tb, ps=ps: e.matmul(
                        ps[:, (2 * tb + c) * 128:(2 * tb + c) * 128 + 128], qhT[:, c, tb * 128:tb * 128 + 128],
                        skT[:, c, :], start=True, stop=True), tq, t_sk, *tf)
            t_sc[h] = S(lambda e, ps=ps: e.activation(sc[h % 2], ps[:, :].rearrange("p (a c n) -> p a c n", a=2, c=2),
                                                      ACT.Copy), m, *sc_free[h % 2])
            put(b, t_sc[h])
            qh_free[0] = [m]

        def peer_topk(h, tb):
            for c in range(2):
                yield from top16(sc[h % 2][:, tb, c, :], sc2[:, c, :], vt[:, c, :], it[:, c, :], t_sc[h], chain[0])
            if tb == 1:
                sc_free[h % 2] = [chain[0]]
            t0 = V(lambda e: e.tensor_copy(itf, it[:, :, :]), chain[0])
            yield
            t1 = V(lambda e: e.tensor_tensor(
                cand.rearrange("p (a b) -> p a b", a=16), vt[:, 0, :].unsqueeze(2).to_broadcast([128, 16, 16]),
                vt[:, 1, :].unsqueeze(1).to_broadcast([128, 16, 16]), ALU.add), chain[0])
            yield
            yield from top16(cand, cand2, ts, pos, t1)
            t2 = chain[0]
            a = V(lambda e: e.tensor_scalar(pi[:, 0, :], pos[:, :], 4, None, ALU.logical_shift_right), t2)
            yield
            b = V(lambda e: e.tensor_scalar(pi[:, 1, :], pos[:, :], 15, None, ALU.bitwise_and), t2)
            yield
            c = V(lambda e: e.tensor_copy(pf, pi[:, :, :]), a, b)
            yield
            for z in range(2):
                d = V(lambda e, z=z: e.tensor_tensor(eq[z], iot[:, :].unsqueeze(1).to_broadcast([128, 16, 16]),
                                                     pf[:, z, :].unsqueeze(2).to_broadcast([128, 16, 16]),
                                                     ALU.is_equal), c, g_i16)
                yield
                f = V(lambda e, z=z: e.tensor_tensor(eq[z], eq[z], itf[:, z, :].unsqueeze(1).to_broadcast([128, 16, 16]),
                                                     ALU.mult), d, t0)
                yield
                f = V(lambda e, z=z: e.tensor_reduce(si[:, z, :], eq[z], AX, ALU.add), f)
                yield
            g = V(lambda e: e.scalar_tensor_tensor(ei, si[:, 0, :], 128.0, si[:, 1, :], ALU.mult, ALU.add), f)
            yield
            t_idx[(h, tb)] = V(lambda e: e.tensor_copy(eidx[:, tb, 16 * h:16 * h + 16], ei), g)
            yield
            gj = gw[:, tb, 16 * h:16 * h + 16]
            a = V(lambda e: e.tensor_scalar(gj, ts, ts[:, 0:1], None, ALU.subtract), t2)
            yield
            x = S(lambda e: e.activation(gj, gj, ACT.Exp, accum_out=smx[:, 0:1]), a)
            a = V(lambda e: e.reciprocal(smx[:, 1:2], smx[:, 0:1]), x)
            yield
            chain[0] = t_gw[(h, tb)] = V(lambda e: e.tensor_scalar(gj, gj, smx[:, 1:2], None, ALU.mult), a)
            yield

        dg2 = sb("dg2", [128, 4, 128])
        dg2_free = [(), (), (), ()]
        dgn = [0]
        t_peer = [None, None]
        NG = 5
        rows = [Bf[j] for j in (6, 7, 8, 9, 10)]
        rows_free = [(mx_last, cols_h[0][1], cols_h[1][1])] * NG
        gn = [0]

        def peer_experts(h, tb):
            for s in range(16 * h, 16 * h + 16, 2):
                dots = []
                for z in range(2):
                    i = gn[0] % NG
                    gn[0] += 1
                    R = rows[i]
                    tg = G.dma(gsem[i], lambda e, z=z, s=s, R=R: e.indirect_dma_start(
                        out=R[:, :], out_offset=None, in_=A["ex"],
                        in_offset=bass.IndirectOffsetOnAxis(ap=eidx[:, tb, s + z:s + z + 1], axis=0)),
                        t_idx[(h, tb)], g_last, *rows_free[i])
                    d = V(lambda e, z=z, s=s, R=R: e.tensor_tensor_reduce(
                        R[:, 0:1024], R[:, 0:1024], XG[:, tb, :], 1.0, 0.0, ALU.mult, ALU.add,
                        av_[:, tb, s + z:s + z + 1]), tg, t_xg[tb])
                    dots.append((i, R, tg, d))
                a = S(lambda e, s=s: e.activation(cf[:, tb, s:s + 2], av_[:, tb, s:s + 2], ACT.Gelu), dots[0][3],
                      dots[1][3])
                b = V(lambda e, s=s: e.tensor_tensor(cf[:, tb, s:s + 2], cf[:, tb, s:s + 2], gw[:, tb, s:s + 2],
                                                     ALU.mult), a, t_gw[(h, tb)])
                for z, (i, R, tg, d) in enumerate(dots):
                    n = dgn[0] % 4
                    dgn[0] += 1
                    c = S(lambda e, n=n, s=s, z=z: e.activation(dg2[:, n, :], ident[:, :], ACT.Copy,
                                                                scale=cf[:, tb, s + z:s + z + 1]), b, *dg2_free[n])
                    for hf in range(2):
                        bi, ps, tf = acc[2 * tb + hf]
                        m = PE(lambda e, n=n, hf=hf, ps=ps, R=R, f=(s + z == 0), l=(s + z == 127): e.matmul(
                            ps[:, :], dg2[:, n, :], R[:, 1024 + 512 * hf:1536 + 512 * hf], start=f, stop=l),
                            c, tg, *tf)
                    dg2_free[n] = (m,)
                    rows_free[i] = (m, d)
                yield
            t_peer[tb] = m

        peer_scores(0, peer_query(0))
        run(peer_topk(0, 0))
        for tb in range(2):
            c, tc = cols_h[tb]
            t_xg.append(V(lambda e, tb=tb, c=c: e.scalar_tensor_tensor(XG[:, tb, :], X[:, tb, :], c, GB[:, :], ALU.mult,
                                                                       ALU.mult), tc, t_gffn, *t_h2, *t_h1))
        t_gfin = S.dma([sem("c_gfin"), 0], lambda e: e.dma_start(GB[:, :], A["gfin"].partition_broadcast(128)), *t_xg)
        debug("eidx", eidx[:, 0, 0:16], *t_idx.values())
        for h in range(8):
            for tb in range(2):
                nxt = iter(())
                if (h, tb) != (7, 1):
                    nxt = peer_topk(h + tb, 1 - tb)
                for n, _ in enumerate(peer_experts(h, tb)):
                    for _ in range(5):
                        next(nxt, None)
                    if tb == 0 and h < 7 and n == 1:
                        tq = peer_query(h + 1)
                    if tb == 0 and h < 7 and n == 3:
                        peer_scores(h + 1, tq)
                run(nxt)
        t_h3 = []
        for tb in range(2):
            for hf in range(2):
                bi, ps, _ = acc[2 * tb + hf]
                t = V(lambda e, tb=tb, hf=hf, ps=ps: e.tensor_tensor(X[:, tb, hf * 512:hf * 512 + 512], ps[:, :],
                                                                     X[:, tb, hf * 512:hf * 512 + 512], ALU.add),
                      t_peer[tb], *t_xg)
                put(bi, t)
                t_h3.append(t)
        debug("h3", X[:, :, :], *t_h3)

        cols_h = norm_cols(X, junk, t_h3, [])
        t_x2 = []
        for tb in range(2):
            c, tc = cols_h[tb]
            t_x2.append(V(lambda e, tb=tb, c=c: e.scalar_tensor_tensor(X[:, tb, :], X[:, tb, :], c, GB[:, :], ALU.mult,
                                                                       ALU.mult), tc, t_gfin, *t_h3))
        debug("x2", X[:, :, :], *t_x2)
        t_ggn = S.dma([sem("c_ggn"), 0], lambda e: e.dma_start(GB[:, :], A["ggn"].partition_broadcast(128)), *t_x2)
        cols_h = norm_cols(X, junk, t_x2, t_x2)
        t_xt = transposed(X, cols_h, gains[:, 4, :], XT, t_x2, [])

        v4_ = lambda ap: ap.rearrange("p (h t) -> p h t", h=4)
        zb, lfb = Bf[0][:, 0:1024], Bf[0][:, 1024:2048]
        et, klT = Bf[1][:, 0:1024], Bf[1][:, 1024:2048]
        qd, kd = Bf[2][:, 0:1024], Bf[2][:, 1024:2048]
        kk_, klt = Bf[3][:, 0:1024], Bf[3][:, 1024:2048]
        b, ps, tf = bank()
        m = prod(ps[0:16, 0:256], lambda a, k: thinr[a][:, k, 8:24], lambda b_, k: XT[b_][:, k, :], range(8), True,
                 True, t_th, *t_xt, *tf)
        glr = sb("glr", [16, 256])
        t = S(lambda e, ps=ps: e.activation(glr[:, :], ps[0:16, 0:256], ACT.Copy), m)
        put(b, t)
        tz = []
        for hp in range(2):
            b, ps, tf = bank()
            for c in range(2):
                h = 2 * hp + c
                m = PE(lambda e, c=c, h=h, ps=ps: e.matmul(ps[:, c * 256:c * 256 + 256], gw2[:, h * 128:h * 128 + 128],
                                                           glr[:, :], start=True, stop=True), t, t_gw2, *tf)
            for c in range(2):
                h = 2 * hp + c
                tt = S(lambda e, c=c, h=h, ps=ps: e.activation(zb[:, h * 256:h * 256 + 256],
                                                               ps[:, c * 256:c * 256 + 256], ACT.Identity,
                                                               bias=gb2[:, h:h + 1]), m, t_gb2, *t_h3)
                tz.append(tt)
            put(b, tt)
        a = S(lambda e: e.activation(lfb, zb, ACT.Abs), *tz)
        x = S(lambda e: e.activation(lfb, lfb, ACT.Exp, scale=-1.0), a)
        x = S(lambda e: e.activation(lfb, lfb, ACT.Ln, bias=1.0), x)
        a = V(lambda e: e.scalar_tensor_tensor(zb, zb, 0.0, lfb, ALU.min, ALU.subtract), x)
        tb_ = V(lambda e: e.tensor_tensor_scan(lfb, scanm[:, :], zb, 0.0, ALU.mult, ALU.add), a, g_scan)
        x1 = S(lambda e: e.activation(et, lfb, ACT.Exp, scale=0.0625), tb_, *t_h3)
        dec = small[:, 16:32]
        l16 = lfb.rearrange("p (c n) -> p c n", n=64)
        t_dec = S(lambda e: e.activation(dec, l16[:, :, 63], ACT.Exp, scale=0.0625), tb_)
        t_qd, t_k = [], []
        run(layer_fm("gq", 0, XT, t_xt, lambda hf, ps, m: V(lambda e: e.scalar_tensor_tensor(
            qd[:, hf * 512:hf * 512 + 512], ps.rearrange("p a b -> p (a b)"), 128.0 ** -0.5,
            et[:, hf * 512:hf * 512 + 512], ALU.mult, ALU.mult), m, x1), t_qd))
        run(layer_fm("gk", 0, XT, t_xt, lambda hf, ps, m: S(lambda e: e.activation(
            kk_[:, hf * 512:hf * 512 + 512], ps.rearrange("p a b -> p (a b)"), ACT.Copy), m), t_k))
        x2 = S(lambda e: e.activation(et, lfb, ACT.Exp, scale=-0.0625), tb_, *t_qd)
        t_kd = V(lambda e: e.tensor_tensor(kd, kk_, et, ALU.mult), x2, *t_k)
        a = V(lambda e: e.tensor_tensor(zb.rearrange("p (c n) -> p c n", n=64),
                                        l16[:, :, 63:64].to_broadcast([128, 16, 64]), l16, ALU.subtract), tb_)
        x3 = S(lambda e: e.activation(zb, zb, ACT.Exp, scale=0.0625), a)
        t_kl = V(lambda e: e.tensor_tensor(klT, kk_, zb, ALU.mult), x3, *t_k)
        gv = Bf[4][:, :].rearrange("p (a d) -> p a d", a=2)
        t_gv = []
        for k in range(2):
            run(layer_tm("gv", k, XT, t_xt, lambda tb, ps, m, k=k: S(
                lambda e: e.activation(gv[:, tb, k * 512:k * 512 + 512], ps[:, :], ACT.Copy), m, *t_h3), t_gv))
        AT = Bf[0][:, 0:512]
        t_at0 = V(lambda e: e.memset(AT, 0.0), x3, t_kl)
        b, ps, tf = bank()
        for h in range(4):
            for n in range(4):
                o = 64 * (n % 2)
                m = PE(lambda e, h=h, n=n, o=o, ps=ps: e.matmul(
                    ps[o:o + 64, (h * 2 + n // 2) * 64:(h * 2 + n // 2) * 64 + 64],
                    kd[:, h * 256 + n * 64:h * 256 + n * 64 + 64], qd[:, h * 256 + n * 64:h * 256 + n * 64 + 64],
                    start=True, stop=True), t_kd, *t_qd, *tf)
        t_at = V(lambda e, ps=ps: e.copy_predicated(AT.rearrange("p (a b) -> p a b", b=64),
                                                    cmask[:, :].bitcast(I32).unsqueeze(1).to_broadcast([128, 8, 64]),
                                                    ps[:, :].rearrange("p (a b) -> p a b", b=64)), m, t_at0, g_cm)
        put(b, t_at)
        t_klt = []
        for tb in range(2):
            b, ps, tf = bank()
            for h in range(4):
                m = PE(lambda e, tb=tb, h=h, ps=ps: e.transpose(
                    ps[:, h * 128:h * 128 + 128], klT[:, h * 256 + tb * 128:h * 256 + tb * 128 + 128], ident[:, :]),
                    t_kl, *tf)
            t = S(lambda e, tb=tb, ps=ps: e.activation(klt[:, tb * 512:tb * 512 + 512], ps[:, :], ACT.Copy), m)
            put(b, t)
            t_klt.append(t)
        SA = [Bf[5][:, 0:1024], Bf[5][:, 1024:2048], Bf[1][:, 0:1024]]
        t_S = {}
        for n in range(3):
            for hp in range(2):
                b, ps, tf = bank()
                o = 64 * (n % 2)
                for c in range(2):
                    h = 2 * hp + c
                    m = PE(lambda e, c=c, h=h, n=n, o=o, ps=ps: e.matmul(
                        ps[:, c * 256:c * 256 + 256],
                        klt[o:o + 64, (n // 2) * 512 + h * 128:(n // 2) * 512 + h * 128 + 128],
                        gv[o:o + 64, n // 2, h * 256:h * 256 + 256], start=True, stop=True), *t_klt, *t_gv, *tf)
                if n == 0:
                    t = V(lambda e, hp=hp, ps=ps: e.tensor_copy(SA[0][:, hp * 512:hp * 512 + 512], ps[:, :]), m)
                else:
                    for c in range(2):
                        h = 2 * hp + c
                        t = V(lambda e, c=c, h=h, n=n, ps=ps: e.scalar_tensor_tensor(
                            SA[n][:, h * 256:h * 256 + 256], SA[n - 1][:, h * 256:h * 256 + 256],
                            dec[:, h * 4 + n:h * 4 + n + 1], ps[:, c * 256:c * 256 + 256], ALU.mult, ALU.add),
                            m, t_dec, t_S[(n - 1, hp)], t_kd)
                put(b, t)
                t_S[(n, hp)] = t
        gr = Bf[6][:, :].rearrange("p (a d) -> p a d", a=2)
        t_gr = []

        def ev_gr(k):
            def ev(tb, ps, m):
                t = S(lambda e: e.activation(gr[:, tb, k * 512:k * 512 + 512], ps[:, :], ACT.Silu), m, *t_h3)
                t_gr.append(V(lambda e: e.tensor_tensor(gr[:, tb, k * 512:k * 512 + 512],
                                                        gr[:, tb, k * 512:k * 512 + 512],
                                                        GB[:, k * 512:k * 512 + 512], ALU.mult), t, t_ggn))
                return t
            return ev

        for k in range(2):
            run(layer_tm("gr", k, XT, t_xt, ev_gr(k)))
        oN = Bf[7][:, :].rearrange("p (a d) -> p a d", a=2)
        t_on = []
        for tb in range(2):
            for hp in range(2):
                b, ps, tf = bank()
                for c in range(2):
                    h = 2 * hp + c
                    for q in range(2):
                        n = 2 * tb + q
                        o = 64 * q
                        m = PE(lambda e, c=c, h=h, n=n, o=o, ps=ps, tb=tb: e.matmul(
                            ps[o:o + 64, c * 256:c * 256 + 256], AT[o:o + 64, (h * 2 + tb) * 64:(h * 2 + tb) * 64 + 64],
                            gv[o:o + 64, tb, h * 256:h * 256 + 256], start=True, stop=(n == 0)), t_at, *t_gv, *tf)
                        if n:
                            m = PE(lambda e, c=c, h=h, n=n, o=o, ps=ps: e.matmul(
                                ps[o:o + 64, c * 256:c * 256 + 256], qd[:, h * 256 + n * 64:h * 256 + n * 64 + 64],
                                SA[n - 1][:, h * 256:h * 256 + 256], start=False, stop=True), t_S[(n - 1, hp)])
                ss = col(2)
                for c in range(2):
                    x = S(lambda e, c=c, ss=ss, ps=ps: e.activation(klT[:, c * 256:c * 256 + 256],
                                                                    ps[:, c * 256:c * 256 + 256], ACT.Square,
                                                                    accum_out=ss[:, c:c + 1]), m, *t_klt)
                r = rstd(ss, 256, x)
                for c in range(2):
                    h = 2 * hp + c
                    t = V(lambda e, c=c, h=h, tb=tb, ss=ss, ps=ps: e.scalar_tensor_tensor(
                        oN[:, tb, h * 256:h * 256 + 256], ps[:, c * 256:c * 256 + 256], ss[:, c:c + 1],
                        gr[:, tb, h * 256:h * 256 + 256], ALU.mult, ALU.mult), r, *t_gr, *t_h3)
                put(b, t)
                t_on.append(t)
        debug("oN", oN, *t_on)
        t_gla_last = m

        BQ = Bf[8][:, :].rearrange("p (k t) -> p k t", k=8)
        BK = Bf[9][:, :].rearrange("p (k t) -> p k t", k=8)
        BV = Bf[2][:, :].rearrange("p (a d) -> p a d", a=2)
        sq = Bf[3][:, 0:2048].rearrange("p (j n) -> p j n", j=4)
        sqn = [0]
        sv = Bf[1][:, 1024:1536]
        sqf = [[t_gla_last, *t_kl_] for t_kl_ in [[t_klt[0]]] * 4]
        t_bn = {"bq": [], "bk": []}

        pend = []

        def ev_bn(name, k, dst, gcol):
            def ev(hf, ps, m):
                c = 4 * k + 2 * hf
                j = sqn[0] % 4
                sqn[0] += 1
                t = S(lambda e: e.activation(dst[:, c:c + 2, :], ps, ACT.Copy), m, *t_xt)
                t2 = S(lambda e: e.activation(sq[:, j, :], dst[:, c:c + 2, :].rearrange("p a b -> p (a b)"),
                                              ACT.Square), t, *sqf[j])
                pend.append((name, c, j, t2, dst, gcol))
                return t
            return ev

        def finish_norm():
            name, c, j, t2, dst, gcol = pend.pop(0)
            b, ps, tf = bank()
            m = PE(lambda e: e.matmul(ps[:, :], ones[:, :], sq[:, j, :], start=True, stop=True), t2, g_on, *tf)
            v = V(lambda e: e.tensor_scalar(sv, ps[:, :], 1.0 / 128, EPS, ALU.mult, ALU.add), m, *sqf[j - 1])
            put(b, v)
            a = S(lambda e: e.activation(sq[:, j, :], sv, ACT.Sqrt), v)
            a = V(lambda e: e.reciprocal(sq[:, j, :], sq[:, j, :]), a)
            f = dst[:, c:c + 2, :].rearrange("p a b -> p (a b)")
            d = V(lambda e: e.scalar_tensor_tensor(f, f, gcol, sq[:, j, :], ALU.mult, ALU.mult), a, t_bqk)
            a = V(lambda e: e.tensor_tensor(sv, sv, sq[:, j, :], ALU.mult), a)
            a = V(lambda e: e.tensor_tensor(sv, sv, sq[:, j, :], ALU.mult), a)
            a = V(lambda e: e.tensor_scalar(sv, sv, -0.5, 1.5, ALU.mult, ALU.add), a)
            a = V(lambda e: e.tensor_tensor(f, f, sv, ALU.mult), a, d)
            sqf[j] = [a]
            t_bn[name].append(a)

        for name, dst, g_ in (("bq", BQ, bqk[:, 0:1]), ("bk", BK, bqk[:, 1:2])):
            for k in range(2):
                run(layer_fm(name, k, XT, t_xt, ev_bn(name, k, dst, g_)))
                while len(pend) > 2:
                    finish_norm()
        t_bv = []
        for k in range(2):
            run(layer_tm("bv", k, XT, t_xt, lambda tb, ps, m, k=k: S(
                lambda e: e.activation(BV[:, tb, k * 512:k * 512 + 512], ps[:, :], ACT.Copy), m, t_gla_last), t_bv))
            if k == 0:
                while pend:
                    finish_norm()
        oT2 = [Br[j][:, :].rearrange("p (k t) -> p k t", k=8) for j in (0, 10)]
        t_oT = transposed(oN, None, None, oT2, t_on, [t_gla_last])
        SGA = Bf[4][:, :].rearrange("p (k t) -> p k t", k=8)
        SGB = Bf[6][:, :].rearrange("p (k t) -> p k t", k=8)
        yT = Bf[5][:, :].rearrange("p (k t) -> p k t", k=8)
        t_ga, t_gb, t_ya = [], [], []
        for k in range(2):
            fills.append(lambda k=k: layer_fm("ga", k, XT, t_xt, lambda hf, ps, m: S(
                lambda e: e.activation(SGA[:, 4 * k + 2 * hf:4 * k + 2 * hf + 2, :], ps, ACT.Sigmoid), m,
                t_gla_last), t_ga))
            fills.append(lambda k=k: layer_fm("gb", k, XT, t_xt, lambda hf, ps, m: S(
                lambda e: e.activation(SGB[:, 4 * k + 2 * hf:4 * k + 2 * hf + 2, :], ps, ACT.Sigmoid), m, *t_on),
                t_gb))
        for k in range(2):
            fills.append(lambda k=k: layer_fm("wa", k, oT2, t_oT, lambda hf, ps, m: V(
                lambda e: e.tensor_tensor(yT[:, 4 * k + 2 * hf:4 * k + 2 * hf + 2, :], ps,
                                          SGA[:, 4 * k + 2 * hf:4 * k + 2 * hf + 2, :], ALU.mult), m, *t_ga,
                t_gla_last), t_ya))
        mT_ = [Br[j][:, :].rearrange("p (k t) -> p k t", k=8) for j in (7, 1)]
        attP = [Bf[3][:, 0:384], Bf[3][:, 384:768]]
        attT = [Bf[3][:, 768:1152], Bf[3][:, 1152:1536]]
        bia = [Bf[3][:, 1536:1792], Bf[3][:, 1792:2048]]
        pfree = [[x for y in sqf for x in y]] * 2
        tfree = [[x for y in sqf for x in y]] * 2
        bfree = [[x for y in sqf for x in y]] * 2
        SC = 128.0 ** -0.5
        t_m = []
        for h in range(10):
            if h < 8:
                bh = bia[h % 2]
                slope = 2.0 ** (-(h + 1))
                tbi = V(lambda e, bh=bh, slope=slope: e.tensor_scalar(bh, DD[:, :], slope / SC, None, ALU.mult), g_dd,
                        *bfree[h % 2])
                b, psS, tf = bank()
                PE(lambda e, psS=psS, h=h: e.matmul(psS[:, 0:128], BQ[:, h, 0:128], BK[:, h, 0:128], start=True,
                                                    stop=True), *t_bn["bq"], *t_bn["bk"], *tf)
                mS = PE(lambda e, psS=psS, h=h: e.matmul(psS[:, 128:384], BQ[:, h, 128:256], BK[:, h, :], start=True,
                                                         stop=True), *t_bn["bq"], *t_bn["bk"], *tf)
                P = attP[h % 2]
                mx, sm = col(2), col(2)
                V(lambda e, P=P, psS=psS, mx=mx, bh=bh: e.tensor_tensor_reduce(
                    P[:, 0:128], psS[:, 0:128], bh[:, 128:256], SC, NEG, ALU.add, ALU.max, mx[:, 0:1]), mS, tbi,
                    *pfree[h % 2])
                r2 = V(lambda e, P=P, psS=psS, mx=mx, bh=bh: e.tensor_tensor_reduce(
                    P[:, 128:384], psS[:, 128:384], bh, SC, NEG, ALU.add, ALU.max, mx[:, 1:2]), mS, tbi,
                    *pfree[h % 2])
                put(b, r2)
                bfree[h % 2] = [r2]
                r3 = V(lambda e, mx=mx: e.tensor_scalar(mx, mx, -1.0, None, ALU.mult), r2)
                for tb, (c0, c1) in enumerate(((0, 128), (128, 384))):
                    x1 = S(lambda e, P=P, c0=c0, c1=c1, tb=tb, mx=mx, sm=sm: e.activation(
                        P[:, c0:c1], P[:, c0:c1], ACT.Exp, bias=mx[:, tb:tb + 1], accum_out=sm[:, tb:tb + 1]), r3)
                r5 = V(lambda e, sm=sm: e.reciprocal(sm, sm), x1)
                V(lambda e, P=P, sm=sm: e.tensor_scalar(P[:, 0:128], P[:, 0:128], sm[:, 0:1], None, ALU.mult), r5)
                r6 = V(lambda e, P=P, sm=sm: e.tensor_scalar(P[:, 128:384], P[:, 128:384], sm[:, 1:2], None, ALU.mult),
                       r5)
                info[h] = (P, r6)
                fill()
            if 1 <= h < 9:
                p = h - 1
                P, tP = info[p]
                b, psT, tf = bank()
                for j in range(3):
                    mT = PE(lambda e, j=j, P=P, psT=psT: e.transpose(psT[:, j * 128:j * 128 + 128],
                                                                     P[:, j * 128:j * 128 + 128], ident[:, :]),
                            tP, *tf)
                PT = attT[p % 2]
                t = S(lambda e, PT=PT, psT=psT: e.activation(PT, psT[:, 0:384], ACT.Copy), mT, *tfree[p % 2])
                put(b, t)
                pfree[p % 2] = (mT,)
                info[p] = (PT, t)
            if h >= 2:
                p = h - 2
                PT, tP = info[p]
                if p % 2 == 0:
                    bV, psV, tfV = bank()
                o = 256 * (p % 2)
                vs = [BV[:, s, p * 128:p * 128 + 128] for s in range(2)]
                PE(lambda e, PT=PT, vs=vs, o=o, psV=psV: e.matmul(psV[:, o:o + 128], vs[0], PT[:, 0:128], start=True,
                                                                  stop=True), tP, *t_bv, *tfV)
                PE(lambda e, PT=PT, vs=vs, o=o, psV=psV: e.matmul(psV[:, o + 128:o + 256], vs[0], PT[:, 128:256],
                                                                  start=True, stop=False), tP)
                mV = PE(lambda e, PT=PT, vs=vs, o=o, psV=psV: e.matmul(psV[:, o + 128:o + 256], vs[1], PT[:, 256:384],
                                                                       start=False, stop=True), tP)
                tfree[p % 2] = (mV,)
                if p % 2 == 1:
                    t = parts(mT_, slice(p - 1, p + 1), psV[:, :].rearrange("p (a b) -> p a b", a=2), mV, *t_oT,
                              *t_bn["bq"], *t_bn["bk"])
                    put(bV, t)
                    t_m.append(t)
        fill(99)
        t_y = []
        tmp = Bf[8][:, :].rearrange("p (k t) -> p k t", k=8)

        yR = [Br[j][:, :].rearrange("p (k t) -> p k t", k=8) for j in (2, 3)]

        def ev_wb(k):
            def ev(hf, ps, m):
                c = 4 * k + 2 * hf
                t = V(lambda e: e.tensor_tensor(tmp[:, c:c + 2, :], ps, SGB[:, c:c + 2, :], ALU.mult), m, *t_gb, mS)
                a = V(lambda e: e.tensor_tensor(yT[:, c:c + 2, :], yT[:, c:c + 2, :], tmp[:, c:c + 2, :], ALU.add), t,
                      *t_ya)
                t_y.append(parts(yR, slice(c, c + 2), yT[:, c:c + 2, :], a, mV))
                return t
            return ev

        for k in range(2):
            run(layer_fm("wb", k, mT_, t_m, ev_wb(k)))
        t_x3 = []
        for k in range(2):
            run(layer_tm("wo2", k, yR, t_y, ev_res(k, t_xt, t_x3)))
            m_w = PE.items[-1][2]
        debug("x3", X[:, :, :], *t_x3)

        junk = Bf[9][:, :].rearrange("p (a d) -> p a d", a=2)
        cols_h = norm_cols(X, junk, t_x3, [mS])
        t_xt = transposed(X, cols_h, gains[:, 5, :], XT, t_x3, [])
        U = [[Br[j + 4 * z][:, :].rearrange("p (k t) -> p k t", k=8) for z in range(2)] for j in range(4)]
        ufree = [*t_y, mV, m_w, *t_x3]
        t_u = {j: [] for j in range(4)}
        rel = [Bf[8][:, 1024 * j:1024 * j + 512].rearrange("p (a b) -> p a b", a=2) for j in range(2)]
        sqr = [Bf[8][:, 1024 * j + 512:1024 * j + 1024].rearrange("p (a b) -> p a b", a=2) for j in range(2)]
        relf = [list(t_y), list(t_y)]

        def ev_up(k):
            def ev(hf, ps, m):
                c = slice(4 * (k % 2) + 2 * hf, 4 * (k % 2) + 2 * hf + 2)
                u, r, q = U[k // 2], rel[hf], sqr[hf]
                t = S(lambda e: e.activation(r, ps, ACT.Relu), m, *relf[hf])
                a = S(lambda e: e.activation(u[0][:, c, :], r, ACT.Square), t, *ufree)
                b = V(lambda e: e.tensor_tensor(q, r, r, ALU.mult), t, *relf[hf])
                b = V(lambda e: e.tensor_tensor(u[1][:, c, :], q, u[0][:, c, :].bitcast(F32), ALU.subtract), a, b,
                      *ufree)
                relf[hf] = [a, b]
                t_u[k // 2].append(b)
                return t
            return ev

        for k in range(8):
            run(layer_fm("up", k, XT, t_xt, ev_up(k)))
        t_x4 = []
        for hf in range(2):
            bk = [bank() for _ in range(2)]
            for r in range(4):
                run(layer_tm("dn", 4 * hf + r, U[r], t_u[r], ev_res(hf, [], t_x4), bk=bk, start=(r == 0),
                             stop=(r == 3)))
        debug("x4", X[:, :, :], *t_x4)

        cols_h = norm_cols(X, junk, t_x4, [])
        t_xt = transposed(X, cols_h, gains[:, 6, :], XT, t_x4, [])
        pT = Bf[8][:, 0:512].rearrange("p (k t) -> p k t", k=2)
        pR = [Br[10][:, 512 * z:512 * z + 512].rearrange("p (k t) -> p k t", k=2) for z in range(2)]
        t_p = S.dma([sem("c_pT"), 0], lambda e: e.dma_start(pT, A["pT"]), *relf[0], *relf[1])
        t_p = parts(pR, slice(0, 2), pT, t_p, *t_ya)
        w, n_, tw = half("ple", 0, 0)
        w = [p[:, :].rearrange("p (k n) -> p k n", k=2) for p in w]
        PW = Bf[5][:, :].rearrange("p (a d) -> p a d", a=2)
        t_pw = []
        for tb in range(2):
            for hf in range(2):
                b, ps, tf = bank()
                m = prod(ps[:, :], lambda a, k, tb=tb: pR[a][:, k, tb * 128:tb * 128 + 128],
                         lambda b_, k, hf=hf, w=w: w[b_][:, k, hf * 512:hf * 512 + 512], range(2), True, True,
                         tw, t_p, *tf)
                t = V(lambda e, tb=tb, hf=hf, ps=ps: e.tensor_copy(PW[:, tb, hf * 512:hf * 512 + 512], ps[:, :]), m,
                      *t_x4)
                put(b, t)
                t_pw.append(t)
        hl_free[n_] = (m,)
        SG = Bf[6][:, :].rearrange("p (a d) -> p a d", a=2)
        s_out = [sem("s_out"), 0]
        t_out = []

        def ev_pg(k):
            def ev(tb, ps, m):
                c = slice(k * 512, k * 512 + 512)
                t = S(lambda e: e.activation(SG[:, tb, c], ps[:, :], ACT.Sigmoid), m, *t_x4)
                a = V(lambda e: e.tensor_tensor(SG[:, tb, c], SG[:, tb, c], PW[:, tb, c], ALU.mult), t, *t_pw)
                a = V(lambda e: e.tensor_tensor(SG[:, tb, c], SG[:, tb, c], X[:, tb, c], ALU.add), a)
                t_out.append(SP.dma(s_out, lambda e: e.dma_start(out[tb * 128:tb * 128 + 128, c], SG[:, tb, c]), a))
                return t
            return ev

        for k in range(2):
            run(layer_tm("pg", k, XT, t_xt, ev_pg(k)))
        SP(lambda e: e.nop(), t_out[-1])

        assert used[0] == len(dma_order)
        if ORDER is None:
            print(dma_order)
        for q in (SP, S, V, PE, G):
            q.number()
        block = ctx.enter_context(nc.Block())

        @block.sync
        def _(e):
            SP.emit(e)

        @block.scalar
        def _(e):
            S.emit(e)

        @block.vector
        def _(e):
            V.emit(e)

        @block.tensor
        def _(e):
            PE.emit(e)

        @block.gpsimd
        def _(e):
            G.emit(e)


def layout(inp):
    def halves(w, kind):
        rows, n = w.shape
        out = []
        for c in range(0, n, 512):
            for r in range(0, rows, 1024):
                t = w[r:r + 1024, c:c + 512].reshape(8, 128, -1).transpose(1, 0, 2)
                if t.shape[2] == 256:
                    out.append(t.reshape(128, 2048))
                elif kind == "f":
                    out += [t[:, :, 0:256].reshape(128, 2048), t[:, :, 256:512].reshape(128, 2048)]
                else:
                    out += [t[:, 0:4, :].reshape(128, 2048), t[:, 4:8, :].reshape(128, 2048)]
        return out

    def cols(v, k):
        return np.ascontiguousarray(v.reshape(k, 128).T)

    g = {k: np.asarray(v) for k, v in inp.items()}
    w = g["w_in"][0]
    aq = w[:, 1544:2056].reshape(1024, 8, 64)[:, [0, 4, 1, 5, 2, 6, 3, 7], :].reshape(1024, 512)
    src = {"qk": w[:, 0:512], "aq": aq, "mv": w[:, 512:1024], "mo": w[:, 1024:1536], "wo1": g["w_out"][0],
           "xq": g["w_xq"][0], "xk": g["w_xk"][0], "xv": g["w_xv"][0], "xo": g["w_xo"][0], "pq": g["w_pq"][0]}
    v = g["w_in_2"][0]
    at = 0
    for name, n in (("gq", 512), ("gk", 512), ("gv", 1024), ("lr", 16), ("gr", 1024), ("bq", 1024), ("bk", 1024),
                    ("bv", 1024), ("ga", 1024), ("gb", 1024)):
        src[name] = v[:, at:at + n]
        at += n
    src |= {"wa": g["w_branch_a_2"][0], "wb": g["w_branch_b_2"][0], "wo2": g["w_out_2"][0], "up": g["w_up_2"][0],
            "dn": g["w_down_2"][0], "pg": g["w_ple_gate_2"][0]}
    src["akv"] = w[:, 2056:2312]
    wt = np.stack([t for name, _, kind in TILES for t in halves(src[name], kind)])
    thin = np.concatenate([w[:, 1536:1544], src["lr"]], axis=1)
    return {
        "x": g["x"][0], "mem": g["mem"][0], "wt": wt,
        "gains": np.stack([cols(g[n].reshape(-1), 8) for n in ("g_mix", "g_mem", "g_cross", "g_ffn", "norm_mix_2",
                                                               "norm_mlp_2", "norm_ple_2")], axis=1),
        "convw": np.ascontiguousarray(g["conv_w"][0].reshape(4, 4, 128).transpose(2, 1, 0)),
        "convb": cols(g["conv_b"][0], 4),
        "bif": np.stack([g["b_igate"][0], g["b_fgate"][0]], axis=1),
        "sinks": g["sinks"][0], "gmh": g["g_mhead"][0], "gffn": g["g_ffn"][0], "gfin": g["g_final"],
        "ggn": g["gla_out_norm_2"].reshape(-1),
        "sk": np.ascontiguousarray(np.stack([g["sub_keys1"][0].T, g["sub_keys2"][0].T], axis=1)),
        "thin": np.ascontiguousarray(thin.reshape(8, 128, 24).transpose(1, 0, 2)),
        "gw2": g["gla_gate_w2_2"][0], "gb2": cols(g["gla_gate_b_2"][0], 4),
        "bqk": np.stack([g["moba_q_norm_2"][0], g["moba_k_norm_2"][0]], axis=1),
        "ex": np.concatenate([g["expert_down"][0], g["expert_up"][0]], axis=1),
        "pT": np.ascontiguousarray(g["p_2"][0, 0].T.reshape(2, 128, 256).transpose(1, 0, 2)),
        "wple": np.ascontiguousarray(g["w_ple_2"][0].reshape(2, 128, 1024).transpose(1, 0, 2)).reshape(128, 2048),
    }


def kernel(**inputs):
    import concourse.bacc as _bacc
    from concourse.bass_utils import run_bass_kernel_spmd as _run

    arrays = layout(inputs)
    nc = _bacc.Bacc("TRN2", target_bir_lowering=False, num_devices=1)
    A = {n: nc.dram_tensor(f"in_{n}", a.shape, F32, kind="ExternalInput").ap() for n, a in arrays.items()}
    out = nc.dram_tensor("out_0", (256, 1024), F32, kind="ExternalOutput").ap()
    program(nc, A, out)
    r = _run(nc, [{f"in_{n}": a for n, a in arrays.items()}], core_ids=[0])
    return r.results[0]["out_0"].reshape(1, 256, 1024)
```

```python
from collections import deque
from contextlib import ExitStack

import numpy as np

import concourse.bass as bass
from concourse import mybir

F32 = mybir.dt.float32
F32R = mybir.dt.float32r
I32 = mybir.dt.int32
U32 = mybir.dt.uint32
ALU = mybir.AluOpType
ACT = mybir.ActivationFunctionType
AX = mybir.AxisListType.X

EPS = 1e-6
NEG = -1e30
RING = 3
NHL = 3

TILES = [("akv", 1, "f"), ("qk", 1, "f"), ("aq", 1, "f"), ("mv", 1, "t"), ("mo", 1, "t"), ("wo1", 2, "t"), ("xq", 2, "f"),
         ("xk", 2, "f"), ("xv", 2, "t"), ("xo", 2, "t"), ("pq", 4, "f"), ("gq", 1, "f"), ("gk", 1, "f"), ("gv", 2, "t"),
         ("gr", 2, "t"), ("bq", 2, "f"), ("bk", 2, "f"), ("bv", 2, "t"), ("ga", 2, "f"), ("gb", 2, "f"), ("wa", 2, "f"),
         ("wb", 2, "f"), ("wo2", 2, "t"), ("up", 8, "f"), ("dn", 8, "t"), ("pg", 2, "t")]
FIRST = {}
_n = 0
for _name, _c, _ in TILES:
    FIRST[_name] = _n
    _n += 1 if _name == "akv" else 2 * _c


def _order():
    o = []
    for name, k in ORDER:
        o += [(name, k, h) for h in range(1 if name in ("akv", "ple") else 2)]
    return o


ORDER = [("akv", 0), ("qk", 0), ("aq", 0), ("mv", 0), ("mo", 0), ("xk", 0), ("xk", 1), ("xv", 0), ("wo1", 0),
         ("wo1", 1), ("xv", 1), ("xq", 0), ("xq", 1), ("xo", 0), ("xo", 1), ("pq", 0), ("pq", 1), ("pq", 2),
         ("pq", 3), ("gq", 0), ("gk", 0), ("gv", 0), ("gv", 1), ("gr", 0), ("bq", 0), ("gr", 1), ("bq", 1),
         ("bk", 0), ("bv", 0), ("bk", 1), ("bv", 1), ("ga", 0), ("gb", 0), ("ga", 1), ("gb", 1), ("wa", 0),
         ("wa", 1), ("wb", 0), ("wb", 1), ("wo2", 0), ("wo2", 1), ("up", 0), ("up", 1), ("up", 2), ("up", 3),
         ("up", 4), ("up", 5), ("up", 6), ("up", 7), ("dn", 0), ("dn", 1), ("dn", 2), ("dn", 3), ("dn", 4),
         ("dn", 5), ("dn", 6), ("dn", 7), ("ple", 0), ("pg", 0), ("pg", 1)]


class Chunks(list):
    pass


class Tok:

    def __init__(self, q, sem=None, value=None):
        self.q, self.sem, self.value, self.used = q, sem, value, sem is not None


class Queue:

    def __init__(self, sem):
        self.sem, self.items = sem, []

    def __call__(self, fn, *waits):
        tok = Tok(self)
        self.items.append((fn, waits, tok))
        for w in waits:
            w.used = True
        return tok

    def dma(self, sem, fn, *waits):
        sem[1] += 16
        tok = Tok(self, sem[0], sem[1])
        self.items.append((fn, waits, tok))
        for w in waits:
            w.used = True
        return tok

    def number(self):
        n = 0
        for _, _, tok in self.items:
            if tok.used and tok.sem is None:
                n += 1
                tok.sem, tok.value = self.sem, n

    def emit(self, eng):
        seen = {}
        for fn, waits, tok in self.items:
            need = {}
            for w in waits:
                k = id(w.sem)
                if w.value > max(seen.get(k, 0), need.get(k, (0, None))[0]):
                    need[k] = (w.value, w.sem)
            for k, (v, s) in need.items():
                eng.wait_ge(s, v)
                seen[k] = v
            ins = fn(eng)
            if tok.sem is not None:
                ins.then_inc(tok.sem, 1 if tok.sem is self.sem else 16)


def program(nc, A, out, dbg=None):
    ctx = ExitStack()
    with ctx:
        def sb(name, shape, dt=F32):
            return ctx.enter_context(nc.sbuf_tensor(name, shape, dt))

        def sem(name):
            return ctx.enter_context(nc.semaphore(name))

        SP, ACTQ, V, PE, G = (Queue(sem(f"s_{n}")) for n in ("sp", "act", "dve", "pe", "pool"))
        S = ACTQ

        ring = sb("ring", [128, RING, 2048])
        rsem = [[sem(f"r{i}"), 0] for i in range(RING)]
        gsem = [[sem(f"g{i}"), 0] for i in range(8)]
        X = sb("X", [128, 2, 1024])
        XT = [sb(f"XT{z}", [128, 8, 256], F32R) for z in range(2)]
        HL = [[sb(f"hl{i}{z}", [128, 2048], F32R) for z in range(2)] for i in range(NHL)]
        with ExitStack() as plain:
            Bf = [plain.enter_context(nc.sbuf_tensor(f"B{i}", [128, 2048], F32)) for i in range(11)]
        Br = [sb(f"R{i}", [128, 2048], F32R) for i in range(11)]
        GB = sb("GB", [128, 1024])
        banks = [ctx.enter_context(nc.psum_tensor(f"ps{i}", [128, 512], F32)) for i in range(8)]
        ident = sb("ident", [128, 128])
        ones = sb("ones", [128, 128])
        M1 = sb("M1", [128, 256])
        DD = sb("DD", [128, 256])
        CT = sb("CT", [128, 128])
        sel = sb("sel", [4, 4, 128])
        cmask = sb("cmask", [128, 64])
        iot = sb("iot", [128, 16])
        ioi = Bf[7][:, 1536:1792].bitcast(I32)
        gains = sb("gains", [128, 7, 8])
        small = sb("small", [128, 64])
        convw = sb("convw", [128, 4, 4])
        convb = sb("convb", [128, 4])
        sinkb = sb("sinkb", [128, 8])
        bif = sb("bif", [4, 2])
        thin = sb("thin", [128, 8, 24])
        thinr = [sb(f"thin{z}", [128, 8, 24], F32R) for z in range(2)]
        gb2 = sb("gb2", [128, 4])
        bqk = sb("bqk", [128, 2])
        skT = sb("skT", [128, 2, 128])
        diags = sb("diags", [128, 4, 128])
        st = sb("st", [128, 256])
        eidx = sb("eidx", [128, 2, 128], I32)
        gw = sb("gw", [128, 2, 128])
        av_ = sb("av_", [128, 2, 128])

        free = deque((i, ()) for i in range(8))

        def bank():
            i, toks = free.popleft()
            return i, banks[i], toks

        def put(i, *toks):
            free.append((i, toks))

        loaded, parted, slot_free, hl_free = [], [], {}, {}
        dma_order, used = [], [0]

        def load_half(n):
            name, k, hf = dma_order[n]
            i = n % RING
            src = A["wple"] if name == "ple" else A["wt"][FIRST[name] + 2 * k + hf]
            loaded.append(SP.dma(rsem[i], lambda e: e.dma_start(ring[:, i, :], src), *slot_free.get(n - RING, ()),
                                 *after))

        def part_half(n):
            i, j = n % RING, n % NHL
            hi, lo = HL[j]
            fr = hl_free.get(n - NHL, ())
            a = S(lambda e: e.activation(hi[:, :], ring[:, i, :], ACT.Copy), loaded[n], *fr)
            b = V(lambda e: e.tensor_tensor(lo[:, :], ring[:, i, :], hi[:, :].bitcast(F32), ALU.subtract), a)
            slot_free[n] = (b,)
            parted.append(b)

        def half(name, k, hf):
            n = used[0]
            used[0] += 1
            if ORDER is None:
                dma_order.append((name, k, hf))
            assert dma_order[n] == (name, k, hf), (n, dma_order[n], name, k, hf)
            ahead(n + NHL if eager[0] else n + 1)
            return HL[n % NHL], n, parted[n]

        eager = [True]
        stop_at, after = [len(ORDER) * 2 if ORDER else 1 << 20], []

        def ahead(upto):
            upto = min(upto, len(dma_order), stop_at[0])
            while len(parted) < upto:
                while len(loaded) < min(len(parted) + RING, len(dma_order), stop_at[0]):
                    load_half(len(loaded))
                part_half(len(parted))

        def preload():
            while len(loaded) < min(len(parted) + RING, len(dma_order), stop_at[0]):
                load_half(len(loaded))

        def done(n, m):
            hl_free[n] = (m,)
            if eager[0] and ORDER is not None:
                ahead(n + NHL + 1)

        if ORDER is not None:
            dma_order = _order()

        sconst = {}

        def cload(dst, src, name, q=SP):
            s = [sem(f"c_{name}"), 0]
            return q.dma(s, lambda e: e.dma_start(dst, src))

        D = {}

        def debug(name, ap, *toks):
            if dbg is not None and name in dbg:
                s = [sem(f"d_{name}"), 0]
                t = SP.dma(s, lambda e: e.dma_start(dbg[name], ap), *toks)
                SP(lambda e: e.nop(), t)

        t_xb = [cload(X[:, tb, :], A["x"][tb * 128:tb * 128 + 128, :], f"x{tb}") for tb in range(2)]
        t_gains = cload(gains[:, :, :], A["gains"], "gains", S)
        g_id0 = G(lambda e: e.memset(ident[:, :], 0.0))
        g_id = G(lambda e: e.affine_select(out=ident[:, :], in_=ident[:, :], compare_op=ALU.not_equal, fill=1.0,
                                           base=0, pattern=[[-1, 128]], channel_multiplier=1), g_id0)
        g_sel0 = G(lambda e: e.memset(sel[:, :, :], 0.0))
        g_sel = G(lambda e: e.affine_select(out=sel[:, :, :], in_=sel[:, :, :], compare_op=ALU.not_equal, fill=1.0,
                                            base=0, pattern=[[-1, 4], [0, 128]], channel_multiplier=1), g_sel0)
        g_m0 = G(lambda e: e.memset(M1[:, :], 0.0))
        g_m1a = G(lambda e: e.affine_select(out=M1[:, 0:128], in_=M1[:, 0:128], compare_op=ALU.is_gt, fill=NEG,
                                            base=0, pattern=[[1, 128]], channel_multiplier=-1), g_m0)
        g_m1 = G(lambda e: e.affine_select(out=M1[:, 128:256], in_=M1[:, 128:256], compare_op=ALU.is_ge, fill=NEG,
                                           base=0, pattern=[[-1, 128]], channel_multiplier=1), g_m0)
        g_ct0 = G(lambda e: e.memset(CT[:, :], 0.0))
        g_ct = G(lambda e: e.affine_select(out=CT[:, :], in_=CT[:, :], compare_op=ALU.is_ge, fill=-NEG,
                                           base=0, pattern=[[1, 128]], channel_multiplier=-1), g_ct0)
        epsc = sb("epsc", [128, 1])
        g_eps = G(lambda e: e.memset(epsc[:, :], EPS))
        S(lambda e: e.activation(small[:, 61:62], epsc[:, :], ACT.Sqrt), g_eps)
        g_on = G(lambda e: e.memset(ones[:, :], 1.0))
        g_io = G(lambda e: e.iota(ioi, pattern=[[1, 256]], base=-128, channel_multiplier=-1))
        g_dd0 = G(lambda e: e.tensor_copy(DD[:, :], ioi), g_io)
        g_dd = G(lambda e: e.affine_select(out=DD[:, :], in_=DD[:, :], compare_op=ALU.is_ge, fill=NEG,
                                           base=128, pattern=[[-1, 256]], channel_multiplier=1), g_dd0)
        g_i16a = G(lambda e: e.iota(ioi[:, 0:16], pattern=[[1, 16]], base=0, channel_multiplier=0), g_dd0)
        g_i16 = G(lambda e: e.tensor_copy(iot[:, :], ioi[:, 0:16]), g_i16a)
        g_c0 = G(lambda e: e.memset(cmask[:, :], 1.0))
        for b in range(2):
            g_cm = G(lambda e, b=b: e.affine_select(out=cmask[64 * b:64 * b + 64, :], in_=cmask[64 * b:64 * b + 64, :],
                                                    compare_op=ALU.is_ge, fill=0.0, base=0, pattern=[[1, 64]],
                                                    channel_multiplier=-1), g_c0)
        g_last = G(lambda e: e.memset(small[:, 60:61], 0.0), g_id, g_sel, g_m1a, g_m1, g_ct, g_on, g_dd, g_i16, g_cm)
        dturn = [0]
        dfree = [(), (), (), ()]
        stat = [0]

        def col(n=1):
            if stat[0] + n > 256:
                stat[0] = 0
            c = stat[0]
            stat[0] += n
            return st[:, c:c + n]

        def rstd(ss, n, *toks):
            w = ss.shape[1]
            v, q = col(w), col(w)
            a = V(lambda e: e.tensor_scalar(v, ss, 1.0 / n, EPS, ALU.mult, ALU.add), *toks)
            b = S(lambda e: e.activation(ss, v, ACT.Sqrt), a)
            b = V(lambda e: e.reciprocal(ss, ss), b)
            a = V(lambda e: e.tensor_tensor(q, v, ss, ALU.mult), b)
            a = V(lambda e: e.tensor_tensor(q, q, ss, ALU.mult), a)
            a = V(lambda e: e.tensor_scalar(q, q, -0.5, 1.5, ALU.mult, ALU.add), a)
            return V(lambda e: e.tensor_tensor(ss, ss, q, ALU.mult), a)

        def norm_cols(src, junk, tsrc, tjunk):
            c = col(2)
            a = S(lambda e: e.activation(junk[:, 0, :], src[:, 0, :], ACT.Square, accum_out=c[:, 0:1]), *tsrc, *tjunk)
            b = V(lambda e: e.tensor_tensor_reduce(junk[:, 1, :], src[:, 1, :], src[:, 1, :], 1.0, 0.0, ALU.mult,
                                                   ALU.add, c[:, 1:2]), *tsrc, *tjunk)
            t = rstd(c, 1024, a, b)
            return [(c[:, 0:1], t), (c[:, 1:2], t), c]

        def diagonals(cols):
            dg = []
            for tb in range(2):
                j = dturn[0] % 4
                dturn[0] += 1
                if cols is None:
                    dg.append((ident[:, :], g_id, None))
                    continue
                c, tc = cols[tb]
                t = V(lambda e, j=j, c=c: e.tensor_scalar(diags[:, j, :], ident[:, :], c, None, ALU.mult), tc, g_id,
                      *dfree[j])
                dg.append((diags[:, j, :], t, j))
            return dg

        def transposed(src, cols, gain, dst, tsrc, tdst, dg=None):
            dg = dg or diagonals(cols)
            res = []
            for k in range(0, 8, 2):
                i, ps, tf = bank()
                for tb in range(2):
                    for kk in range(2):
                        m = PE(lambda e, k=k, kk=kk, tb=tb, ps=ps: e.matmul(
                            ps[:, kk * 256 + tb * 128:kk * 256 + tb * 128 + 128],
                            src[:, tb, (k + kk) * 128:(k + kk + 1) * 128], dg[tb][0], start=True, stop=True),
                            *tf, *tsrc, dg[tb][1])
                if gain is None:
                    t = parts(dst, slice(k, k + 2), ps[:, :].rearrange("p (a b) -> p a b", a=2), m, *tdst)
                else:
                    for kk in range(2):
                        a = S(lambda e, k=k + kk, p_=ps[:, kk * 256:kk * 256 + 256]: e.activation(
                            dst[0][:, k, :], p_, ACT.Copy, scale=gain[:, k:k + 1]), m, *tdst, t_gains)
                    for kk in range(2):
                        t = V(lambda e, k=k + kk, p_=ps[:, kk * 256:kk * 256 + 256]: e.scalar_tensor_tensor(
                            dst[1][:, k, :], p_, gain[:, k:k + 1], dst[0][:, k, :].bitcast(F32), ALU.mult,
                            ALU.subtract), m, a, *tdst, t_gains)
                put(i, t)
                res.append(t)
            for _, _, j in dg:
                if j is not None:
                    dfree[j] = (m,)
            return Chunks(res)

        def turned(k0, gain, tsrc):
            res = []
            for k in range(k0, k0 + 4, 2):
                i, ps, tf = bank()
                for tb in range(2):
                    for kk in range(2):
                        m = PE(lambda e, k=k, kk=kk, tb=tb, ps=ps: e.transpose(
                            ps[:, kk * 256 + tb * 128:kk * 256 + tb * 128 + 128],
                            X[:, tb, (k + kk) * 128:(k + kk + 1) * 128], ident[:, :]), *tf, tsrc[tb], g_id)
                for kk in range(2):
                    a = S(lambda e, k=k + kk, p_=ps[:, kk * 256:kk * 256 + 256]: e.activation(
                        XT[0][:, k, :], p_, ACT.Copy, scale=gain[:, k:k + 1]), m, t_gains)
                for kk in range(2):
                    t = V(lambda e, k=k + kk, p_=ps[:, kk * 256:kk * 256 + 256]: e.scalar_tensor_tensor(
                        XT[1][:, k, :], p_, gain[:, k:k + 1], XT[0][:, k, :].bitcast(F32), ALU.mult,
                        ALU.subtract), m, a, t_gains)
                put(i, t)
                res.append(t)
            return res

        def into_next(gen, gain, res, more=lambda: None, last=lambda: None):
            next(gen)
            t_xt = Chunks(turned(0, gain, res[0:2]))
            eager[0] = False
            run(gen)
            more()
            t_xt.extend(turned(4, gain, res[2:4]))
            last()
            return t_xt

        def parts(dst, c, src, *toks):
            a = S(lambda e: e.activation(dst[0][:, c, :], src, ACT.Copy), *toks)
            return V(lambda e: e.tensor_tensor(dst[1][:, c, :], src, dst[0][:, c, :].bitcast(F32), ALU.subtract),
                     a, *toks)

        TERMS = [(0, 0), (0, 1), (1, 0)]

        def prod(ps, lhs, rhs, ks, start=True, stop=True, *toks, per={}, base=0):
            ks = list(ks)
            for g in range(0, len(ks), 4):
                for a, b in TERMS:
                    for k in ks[g:g + 4]:
                        m = PE(lambda e, a=a, b=b, k=k, x=lhs(a, k), y=rhs(b, k): e.matmul(
                            ps, x, y, start=start and (a, b, k) == (0, 0, ks[0]),
                            stop=stop and (a, b, k) == (1, 0, ks[-1])), *toks, *per.get(k + base, ()))
            return m

        def by_chunk(tsrc):
            if isinstance(tsrc, Chunks):
                return (), {k: (tsrc[k // 2],) for k in range(8)}
            return tsrc, {}

        def layer_fm(name, k, src, tsrc, evac, res=None):
            ts, per = by_chunk(tsrc)
            for hf in range(2):
                w, n, tw = half(name, k, hf)
                w = [p[:, :].rearrange("p (k n) -> p k n", k=8) for p in w]
                b, ps, tf = bank()
                for c in range(2):
                    m = prod(ps[:, c * 256:c * 256 + 256], lambda a, k, c=c: w[a][:, k, c * 128:c * 128 + 128],
                             lambda b_, k: src[b_][:, k, :], range(8), True, True, tw, *ts, *tf, per=per)
                t = evac(hf, ps[:, :].rearrange("p (a b) -> p a b", a=2), m)
                put(b, t)
                done(n, m)
                if res is not None:
                    res.append(t)
                yield

        def layer_tm(name, k, src, tsrc, evac, res=None, bk=None, start=True, stop=True):
            ts, per = by_chunk(tsrc)
            own = bk is None
            bk = [bank() for _ in range(2)] if own else bk
            for hf in range(2):
                w, n, tw = half(name, k, hf)
                w = [p[:, :].rearrange("p (k n) -> p k n", k=4) for p in w]
                for tb in range(2):
                    m = prod(bk[tb][1][:, :], lambda a, k, tb=tb, hf=hf: src[a][:, 4 * hf + k, tb * 128:tb * 128 + 128],
                             lambda b_, k: w[b_][:, k, :], range(4), start and hf == 0, stop and hf == 1,
                             tw, *ts, *bk[tb][2], per=per, base=4 * hf)
                    if hf == 1 and stop:
                        t = evac(tb, bk[tb][1], m)
                        put(bk[tb][0], t)
                        if res is not None:
                            res.append(t)
                done(n, m)
                yield

        def run(*gens):
            for g in gens:
                for _ in g:
                    pass

        fills = deque()

        def fill(n=1):
            while n and fills:
                if callable(fills[0]):
                    fills[0] = fills[0]()
                if next(fills[0], fills) is fills:
                    fills.popleft()
                else:
                    n -= 1

        def fill_late():
            eager[0] = False
            fill()
            eager[0] = True

        def late_splits():
            if ORDER is not None:
                ahead(used[0] + NHL)

        junk = Bf[9][:, :].rearrange("p (a d) -> p a d", a=2)
        preload()
        cols_x = norm_cols(X, junk, t_xb, [])
        dg_x = diagonals(cols_x)
        ahead(1)
        t_cw = cload(convw[:, :, :], A["convw"], "convw", S)
        t_cb = cload(convb[:, :], A["convb"], "convb", S)
        t_bif = cload(bif[:, :], A["bif"], "bif", S)
        t_sink = cload(sinkb[:, :], A["sinks"].partition_broadcast(128), "sinks", S)
        t_gm = cload(GB[:, 0:512], A["gmh"].partition_broadcast(128), "gmh", S)
        t_sk = cload(skT[:, :, :], A["sk"], "sk", S)
        t_thin = cload(thin[:, :, :], A["thin"], "thin", S)
        t_mem = cload(Bf[0][:, :].rearrange("p (a d) -> p a d", a=2),
                      A["mem"].rearrange("(a p) d -> p a d", p=128), "mem", S)
        t_gb2 = cload(gb2[:, :], A["gb2"], "gb2", S)
        t_bqk = cload(bqk[:, :], A["bqk"], "bqk", S)

        t_xt = transposed(X, cols_x, gains[:, 0, :], XT, t_xb, [], dg_x)

        akT = Bf[3][:, 1024:1280]
        avt = Bf[3][:, 1280:1536].rearrange("p (a d) -> p a d", a=2)
        bK, psK, tf = bank()
        wk, n_, tw = half("akv", 0, 0)
        wk = [p[:, :].rearrange("p (k n) -> p k n", k=8) for p in wk]
        ts, per = by_chunk(t_xt)
        prod(psK[:, 0:256], lambda a, k: wk[a][:, k, 0:128], lambda b_, k: XT[b_][:, k, :], range(8), True, True,
             tw, *ts, *tf, per=per)
        for tb in range(2):
            m2 = prod(psK[:, 256 + tb * 128:384 + tb * 128],
                      lambda a, k, tb=tb: XT[a][:, k, tb * 128:tb * 128 + 128],
                      lambda b_, k: wk[b_][:, k, 128:256], range(8), True, True, tw, *t_xt, *tf)
        done(n_, m2)
        t_ak = S(lambda e: e.activation(akT, psK[:, 0:256], ACT.Copy), m2)
        t_av = S(lambda e: e.activation(avt, psK[:, 256:512].rearrange("p (a d) -> p a d", a=2), ACT.Copy), m2)
        put(bK, t_av)

        t_th = S(lambda e: e.activation(thinr[0][:, :, :], thin[:, :, :], ACT.Copy), t_thin)
        t_th = V(lambda e: e.tensor_tensor(thinr[1][:, :, :], thin[:, :, :], thinr[0][:, :, :].bitcast(F32),
                                           ALU.subtract), t_th, g_last)
        qkT = Bf[2][:, 0:1024].rearrange("p (a t) -> p a t", a=4)
        yv = Bf[2][:, 1024:2048].rearrange("p (a t) -> p a t", a=4)
        t_qk = []

        def ev_conv(hf, ps, m):
            for c in range(2):
                ch = 2 * hf + c
                t = V(lambda e, ch=ch, c=c: e.tensor_scalar(yv[:, ch, :], ps[:, c, :], convw[:, ch, 3:4],
                                                            convb[:, ch:ch + 1], ALU.mult, ALU.add), m, t_cw, t_cb)
                for s in range(1, 4):
                    t = V(lambda e, ch=ch, c=c, s=s: e.scalar_tensor_tensor(
                        yv[:, ch, s:256], ps[:, c, 0:256 - s], convw[:, ch, 3 - s:4 - s], yv[:, ch, s:256],
                        ALU.mult, ALU.add), t)
                t_qk.append(S(lambda e, ch=ch: e.activation(qkT[:, ch, :], yv[:, ch, :], ACT.Silu), t))
            return t

        run(layer_fm("qk", 0, XT, t_xt, ev_conv))
        debug("qkT", qkT, *t_qk)
        bG, psG, tf = bank()
        for tb in range(2):
            mg = prod(psG[:, 8 * tb:8 * tb + 8], lambda a, k, tb=tb: XT[a][:, k, tb * 128:tb * 128 + 128],
                      lambda b_, k: thinr[b_][:, k, 0:8], range(8), True, True, t_th, *t_xt, *tf)
        gtk = small[:, 32:48]
        t = S(lambda e, ps=psG: e.activation(gtk, ps[:, 0:16], ACT.Copy), mg)
        put(bG, t)
        aqT = Bf[3][:, 0:1024].rearrange("p (a t) -> p a t", a=4)
        t_aq = []
        run(layer_fm("aq", 0, XT, t_xt, lambda hf, ps, m: S(
            lambda e: e.activation(aqT[:, 2 * hf:2 * hf + 2, :], ps, ACT.Copy), m), t_aq))

        bG, psH, tf = bank()
        for z in range(2):
            for tb in range(2):
                mg = PE(lambda e, z=z, tb=tb: e.transpose(psH[0:4, z * 256 + tb * 128:z * 256 + tb * 128 + 128],
                                                          gtk[:, 8 * tb + 4 * z:8 * tb + 4 * z + 4], ident[:, :]),
                        t, g_id, *tf)
        gt = Bf[4][0:4, 0:2048].rearrange("p (a b) -> p a b", b=256)
        ip, z_, ab, lf, bb, aa, MM, mm_ = (gt[:, j, :] for j in range(8))
        v1 = V(lambda e: e.tensor_scalar(ip, psH[0:4, 0:256], bif[:, 0:1], None, ALU.add), mg, t_bif)
        v2 = V(lambda e: e.tensor_scalar(z_, psH[0:4, 256:512], bif[:, 1:2], None, ALU.add), mg, t_bif)
        put(bG, v2)
        v3 = S(lambda e: e.activation(ab, z_, ACT.Abs), v2)
        a1 = S(lambda e: e.activation(ab, ab, ACT.Exp, scale=-1.0), v3)
        a2 = S(lambda e: e.activation(ab, ab, ACT.Ln, bias=1.0), a1)
        v4 = V(lambda e: e.scalar_tensor_tensor(lf, z_, 0.0, ab, ALU.min, ALU.subtract), a2)
        g_o4 = V(lambda e: e.memset(mm_, 1.0))
        v5 = V(lambda e: e.tensor_tensor_scan(bb, mm_, lf, 0.0, ALU.mult, ALU.add), v4, g_o4)
        v6 = V(lambda e: e.tensor_tensor(aa, ip, bb, ALU.subtract), v5, v1)
        v6b = V(lambda e: e.memset(z_, 0.0), v4)
        v7 = V(lambda e: e.tensor_tensor_scan(MM, z_, aa, 0.0, ALU.add, ALU.max), v6, v6b)
        v8 = V(lambda e: e.tensor_tensor(mm_, bb, MM, ALU.add), v7)

        V1 = Bf[7][:, 0:1032].rearrange("p (a h d) -> p a h d", a=2, h=4)
        t_v1o = V(lambda e: e.memset(V1[:, :, :, 128:129], 1.0))
        t_mv = []
        run(layer_tm("mv", 0, XT, t_xt, lambda tb, ps, m: S(
            lambda e: e.activation(V1[:, tb, :, 0:128], ps[:, :].rearrange("p (h d) -> p h d", h=4), ACT.Copy), m),
            t_mv))
        mem = Bf[0][:, :].rearrange("p (a d) -> p a d", a=2)
        cols_m = norm_cols(mem, junk, [t_mem], t_xt)
        dg_m = diagonals(cols_m)
        og = Bf[5][:, 0:1024].rearrange("p (a d) -> p a d", a=2)

        def ev_mo(tb, ps, m):
            t = S(lambda e: e.activation(og[:, tb, :], ps[:, :], ACT.Sigmoid), m)
            D[f"og{tb}"] = V(lambda e: e.tensor_tensor(og[:, tb, :], og[:, tb, :], GB[:, 0:512], ALU.mult), t, t_gm)
            return t

        run(layer_tm("mo", 0, XT, t_xt, ev_mo))
        t_og = [D["og0"], D["og1"]]

        bA, psA, tf = bank()
        for tb in range(2):
            for z, src in enumerate((aa, mm_)):
                mt = PE(lambda e, tb=tb, z=z, src=src: e.transpose(psA[:, 8 * tb + 4 * z:8 * tb + 4 * z + 4],
                                                                   src[:, tb * 128:tb * 128 + 128], ident[0:4, 0:4]),
                        v8, g_id, *tf)
        ac = small[:, 0:8].rearrange("p (a h) -> p a h", a=2)
        em = small[:, 8:16].rearrange("p (a h) -> p a h", a=2)
        p4 = psA[:, 0:16].rearrange("p (a z h) -> p a z h", a=2, z=2)
        t_ac = S(lambda e: e.activation(ac, p4[:, :, 0, :], ACT.Copy), mt)
        t_em = S(lambda e: e.activation(em, p4[:, :, 1, :], ACT.Exp, scale=-1.0), mt)
        put(bA, t_em)

        memT = [Br[j][:, :].rearrange("p (k t) -> p k t", k=8) for j in (1, 10)]
        KT = Bf[8][:, :].rearrange("p (k t) -> p k t", k=8)
        VX = Bf[6][:, :].rearrange("p (a d) -> p a d", a=2)
        t_mT, t_kx, t_vx = [], [], []

        def mem_transposed():
            t_mT.extend(transposed(mem, cols_m, gains[:, 1, :], memT, [t_mem], [], dg_m))
            yield

        fills.append(mem_transposed)
        for k in range(2):
            fills.append(lambda k=k: layer_fm("xk", k, memT, t_mT, lambda hf, ps, m: S(
                lambda e: e.activation(KT[:, 4 * k + 2 * hf:4 * k + 2 * hf + 2, :], ps, ACT.Copy), m), t_kx))
        for k in range(2):
            fills.append(lambda k=k: layer_tm("xv", k, memT, t_mT, lambda tb, ps, m: S(
                lambda e: e.activation(VX[:, tb, k * 512:k * 512 + 512], ps[:, :], ACT.Copy), m), t_vx))
        hm = Bf[5][:, 1024:2048].rearrange("p (a d) -> p a d", a=2)
        dbuf = [Bf[9][:, 0:384], Bf[9][:, 384:768]]
        gbuf = [Bf[9][:, 768 + 384 * j:1152 + 384 * j] for j in range(3)]
        fill(1)
        gfree = [tuple(cols_m[j][1] for j in range(2))] * 3
        Gt = {}
        ssh = col(8)
        t_h = []
        for h in range(6):
            if h < 4:
                po = 64 * (h % 2)
                qh, kh = qkT[po:po + 64, h // 2, :], qkT[po:po + 64, 2 + h // 2, :]
                bM, psM, tf = bank()
                mM = PE(lambda e, h=h, psM=psM: e.matmul(psM[:, 0:256], sel[:, h, :], MM, start=True, stop=True),
                        v8, g_sel, *tf)
                d, g = dbuf[h % 2], gbuf[h % 3]
                fr = gfree[h % 3] + tuple(Gt[x][1] for x in (h - 2,) if x in Gt)
                e1 = V(lambda e, d=d, psM=psM: e.tensor_tensor(d[:, 0:128], psM[:, 0:128], CT[:, :], ALU.add),
                       mM, g_ct, *fr)
                e2 = V(lambda e, d=d, psM=psM: e.tensor_tensor(d[:, 256:384], psM[:, 128:256], CT[:, :], ALU.add),
                       mM, g_ct, *fr)
                e3 = V(lambda e, d=d, psM=psM: e.tensor_copy(d[:, 128:256], psM[:, 128:256]), mM, *fr)
                put(bM, e3)
                x1 = S(lambda e, d=d, h=h: e.activation(d[:, 0:256], d[:, 0:256], ACT.Exp, scale=-1.0,
                                                        bias=ac[:, 0, h:h + 1]), e3, t_ac)
                x2 = S(lambda e, d=d, h=h: e.activation(d[:, 256:384], d[:, 256:384], ACT.Exp, scale=-1.0,
                                                        bias=ac[:, 1, h:h + 1]), e3, t_ac)
                bS, psS, tf = bank()
                PE(lambda e, psS=psS, kh=kh, qh=qh: e.matmul(psS[:, 0:256], kh[:, 0:128], qh, start=True, stop=True),
                   *t_qk, *tf)
                mS = PE(lambda e, psS=psS, kh=kh, qh=qh: e.matmul(psS[:, 256:384], kh[:, 128:256], qh[:, 128:256],
                                                                  start=True, stop=True), *t_qk, *tf)
                tg = V(lambda e, g=g, psS=psS, d=d: e.scalar_tensor_tensor(g, psS[:, 0:384], 0.125, d, ALU.mult,
                                                                           ALU.mult), mS, x1, x2, *fr)
                put(bS, tg)
                Gt[h] = (g, tg)
                late_splits()
                if h < 3:
                    fill_late()
            if h >= 2:
                p = h - 2
                g, tg = Gt[p]
                bO, psO, tf = bank()
                PE(lambda e, g=g, p=p, psO=psO: e.matmul(psO[:, 0:129], g[:, 0:128], V1[:, 0, p, :], start=True,
                                                         stop=True), tg, *t_mv, t_v1o, *tf)
                PE(lambda e, g=g, p=p, psO=psO: e.matmul(psO[:, 129:258], g[:, 128:256], V1[:, 0, p, :], start=True,
                                                         stop=False), tg)
                mO = PE(lambda e, g=g, p=p, psO=psO: e.matmul(psO[:, 129:258], g[:, 256:384], V1[:, 1, p, :],
                                                              start=False, stop=True), tg)
                gfree[p % 3] = (mO,)
                dn = col(2)
                n1 = S(lambda e, dn=dn, psO=psO: e.activation(
                    dn, psO[:, 0:258].rearrange("p (a d) -> p a d", a=2)[:, :, 128], ACT.Abs), mO)
                n2 = V(lambda e, dn=dn, p=p: e.tensor_tensor(dn, dn, em[:, :, p], ALU.max), n1, t_em)
                n3 = V(lambda e, dn=dn: e.reciprocal(dn, dn), n2)
                for tb in range(2):
                    n4 = V(lambda e, dn=dn, tb=tb, p=p, psO=psO: e.tensor_scalar(
                        hm[:, tb, p * 128:p * 128 + 128], psO[:, tb * 129:tb * 129 + 128], dn[:, tb:tb + 1], None,
                        ALU.mult), n3)
                    t_h.append(S(lambda e, tb=tb, p=p: e.activation(
                        Bf[2][:, 1536 + tb * 128:1664 + tb * 128], hm[:, tb, p * 128:p * 128 + 128], ACT.Square,
                        accum_out=ssh[:, tb * 4 + p:tb * 4 + p + 1]), n4, *t_h[-1:], *t_qk))
                put(bO, n4)
        trs = rstd(ssh, 128, *t_h)
        for tb in range(2):
            for p in range(4):
                tn = V(lambda e, tb=tb, p=p: e.scalar_tensor_tensor(
                    hm[:, tb, p * 128:p * 128 + 128], hm[:, tb, p * 128:p * 128 + 128],
                    ssh[:, tb * 4 + p:tb * 4 + p + 1], og[:, tb, p * 128:p * 128 + 128], ALU.mult, ALU.mult),
                    trs, *t_og)
        debug("hm", hm, tn)
        t_gffn = S.dma([sem("c_gffn"), 0], lambda e: e.dma_start(GB[:, :], A["gffn"].partition_broadcast(128)), *t_og)

        mixT = [Br[j][:, :].rearrange("p (k t) -> p k t", k=8) for j in (0, 4)]

        attP = [Bf[9][:, 384 * j:384 * j + 384] for j in range(3)]
        attT = [Bf[9][:, 1152 + 384 * j:1536 + 384 * j] for j in range(2)]
        pfree = [gfree[0] + gfree[1] + gfree[2]] * 3
        tfree = [gfree[0] + gfree[1] + gfree[2]] * 2
        info = {}
        t_mix, t_hmix = [], []
        for h in range(11):
            if h < 8:
                po = 64 * (h // 4)
                qh, kh = aqT[po:po + 64, h % 4, :], akT[po:po + 64, :]
                bS, psS, tf = bank()
                PE(lambda e, psS=psS, kh=kh, qh=qh: e.matmul(psS[:, 0:128], qh[:, 0:128], kh[:, 0:128], start=True,
                                                             stop=True), *t_aq, t_ak, *tf)
                mS = PE(lambda e, psS=psS, kh=kh, qh=qh: e.matmul(psS[:, 128:384], qh[:, 128:256], kh, start=True,
                                                                  stop=True), *t_aq, t_ak, *tf)
                P = attP[h % 3]
                mx = col(2)
                sm = col(2)
                V(lambda e, P=P, psS=psS, mx=mx: e.tensor_tensor_reduce(P[:, 0:128], psS[:, 0:128], M1[:, 128:256],
                                                                        0.125, NEG, ALU.add, ALU.max, mx[:, 0:1]),
                  mS, g_m1, g_m1a, *pfree[h % 3])
                r2 = V(lambda e, P=P, psS=psS, mx=mx: e.tensor_tensor_reduce(P[:, 128:384], psS[:, 128:384], M1[:, :],
                                                                             0.125, NEG, ALU.add, ALU.max, mx[:, 1:2]),
                       mS, g_m1, g_m1a, *pfree[h % 3])
                put(bS, r2)
                r3 = V(lambda e, mx=mx, h=h: e.tensor_scalar(mx, mx, sinkb[:, h:h + 1], -1.0, ALU.max, ALU.mult), r2,
                       t_sink)
                for tb, (c0, c1) in enumerate(((0, 128), (128, 384))):
                    x1 = S(lambda e, P=P, c0=c0, c1=c1, tb=tb, mx=mx, sm=sm: e.activation(
                        P[:, c0:c1], P[:, c0:c1], ACT.Exp, bias=mx[:, tb:tb + 1], accum_out=sm[:, tb:tb + 1]), r3)
                es = col(2)
                x3 = S(lambda e, es=es, mx=mx, h=h: e.activation(es, mx, ACT.Exp, bias=sinkb[:, h:h + 1]), r3)
                info[h] = (P, sm, es, x1, x3)
            if h == 3:
                for c in range(0, 4, 2):
                    b, ps, tf = bank()
                    for cc in range(2):
                        for tb in range(2):
                            m = PE(lambda e, c=c, cc=cc, tb=tb, ps=ps: e.transpose(
                                ps[:, cc * 256 + tb * 128:cc * 256 + tb * 128 + 128],
                                hm[:, tb, (c + cc) * 128:(c + cc + 1) * 128], ident[:, :]), tn, g_id, *tf)
                    t = parts(mixT, slice(c, c + 2), ps[:, :].rearrange("p (a b) -> p a b", a=2), m, *t_mT, mM)
                    put(b, t)
                    t_hmix.append(t)
            if 1 <= h < 9:
                p = h - 1
                P, sm, es, x1, x3 = info[p]
                r4 = V(lambda e, sm=sm, es=es: e.tensor_tensor(sm, sm, es, ALU.add), x1, x3)
                r5 = V(lambda e, sm=sm: e.reciprocal(sm, sm), r4)
                V(lambda e, P=P, sm=sm: e.tensor_scalar(P[:, 0:128], P[:, 0:128], sm[:, 0:1], None, ALU.mult), r5)
                r6 = V(lambda e, P=P, sm=sm: e.tensor_scalar(P[:, 128:384], P[:, 128:384], sm[:, 1:2], None, ALU.mult),
                       r5)
                info[p] = (P, r6)
            late_splits()
            if h in (0, 2, 4):
                fill_late()
            if 2 <= h < 10:
                p = h - 2
                P, tP = info[p]
                bT, psT, tf = bank()
                for j in range(3):
                    mT = PE(lambda e, j=j, P=P, psT=psT: e.transpose(psT[:, j * 128:j * 128 + 128],
                                                                     P[:, j * 128:j * 128 + 128], ident[:, :]),
                            tP, g_id, *tf)
                PT = attT[p % 2]
                t = S(lambda e, PT=PT, psT=psT: e.activation(PT, psT[:, 0:384], ACT.Copy), mT, *tfree[p % 2])
                put(bT, t)
                pfree[p % 3] = (mT,)
                info[p] = (PT, t)
            if h >= 3:
                p = h - 3
                PT, tP = info[p]
                kv = p // 4
                if p % 2 == 0:
                    bV, psV, tfV = bank()
                po = 64 * (p % 2)
                vs = [avt[:, s, kv * 64:kv * 64 + 64] for s in range(2)]
                PE(lambda e, PT=PT, vs=vs, po=po, psV=psV: e.matmul(psV[po:po + 64, 0:128], vs[0], PT[:, 0:128],
                                                                    start=True, stop=True), tP, t_av, *tfV)
                PE(lambda e, PT=PT, vs=vs, po=po, psV=psV: e.matmul(psV[po:po + 64, 128:256], vs[0], PT[:, 128:256],
                                                                    start=True, stop=False), tP)
                mV = PE(lambda e, PT=PT, vs=vs, po=po, psV=psV: e.matmul(psV[po:po + 64, 128:256], vs[1],
                                                                         PT[:, 256:384], start=False, stop=True), tP)
                tfree[p % 2] = (mV,)
                if p % 2 == 1:
                    t = parts(mixT, slice(4 + p // 2, 5 + p // 2), psV[:, 0:256].unsqueeze(1), mV, *t_mT, mM)
                    put(bV, t)
                    t_mix.append(t)
        t_mix = Chunks([t_hmix[0], t_hmix[1], t_mix[1], t_mix[3]])

        def ev_res(k, tx, res):
            def ev(tb, ps, m):
                t = V(lambda e: e.tensor_tensor(X[:, tb, k * 512:k * 512 + 512], ps[:, :],
                                                X[:, tb, k * 512:k * 512 + 512], ALU.add), m, *tx)
                res.append(t)
                return t
            return ev

        t_h1 = []

        def filler():
            eager[0] = True
            fill(1)

        run(layer_tm("wo1", 0, mixT, t_mix, ev_res(0, t_xt, t_h1)))
        t_xt = into_next(layer_tm("wo1", 1, mixT, t_mix, ev_res(1, t_xt, t_h1)), gains[:, 2, :], t_h1,
                         filler, lambda: fill(99))
        debug("h1", X[:, :, :], *t_h1)

        cols_h = norm_cols(X, junk, t_h1, [mV])
        eager[0] = True
        ahead(used[0] + NHL)
        rs, rn = col(2), col(2)
        t_rs = V(lambda e, c=cols_h[2]: e.tensor_scalar(rs, c, 0.0625, None, ALU.mult), cols_h[0][1])
        t_rn = V(lambda e, c=cols_h[2]: e.tensor_scalar(rn, c, -0.0625, None, ALU.mult), cols_h[0][1])
        QT = Bf[2][:, :].rearrange("p (k t) -> p k t", k=8)
        t_qx = []
        for k in range(2):
            run(layer_fm("xq", k, XT, t_xt, lambda hf, ps, m, k=k: S(
                lambda e: e.activation(QT[:, 4 * k + 2 * hf:4 * k + 2 * hf + 2, :], ps, ACT.Copy), m), t_qx))
        oT = [Br[j][:, :].rearrange("p (k t) -> p k t", k=8) for j in (3, 7)]
        attP = [Bf[9][:, 512 * j:512 * j + 512] for j in range(3)]
        attT = [Bf[10][:, 512 * j:512 * j + 512] for j in range(2)]
        pfree = [t_xt] * 3
        tfree = [t_xt + t_vx + t_kx] * 2
        t_o = []
        for h in range(7):
            if h < 4:
                b, ps, tf = bank()
                for tb in range(2):
                    for kk in range(2):
                        m = PE(lambda e, h=h, tb=tb, kk=kk, ps=ps: e.matmul(
                            ps[:, tb * 256:tb * 256 + 256], QT[:, 2 * h + kk, tb * 128:tb * 128 + 128],
                            KT[:, 2 * h + kk, :], start=(kk == 0), stop=(kk == 1)), *t_qx, *t_kx, *tf)
                P = attP[h % 3]
                mx, sm = col(2), col(2)
                r1 = V(lambda e, mx=mx, ps=ps: e.tensor_reduce(mx, ps[:, :].rearrange("p (a b) -> p a b", a=2), AX,
                                                               ALU.max), m)
                r2 = V(lambda e, mx=mx: e.tensor_tensor(mx, mx, rn, ALU.mult), r1, t_rn)
                for tb in range(2):
                    x = S(lambda e, tb=tb, P=P, ps=ps, mx=mx, sm=sm: e.activation(
                        P[:, tb * 256:tb * 256 + 256], ps[:, tb * 256:tb * 256 + 256], ACT.Exp, scale=rs[:, tb:tb + 1],
                        bias=mx[:, tb:tb + 1], accum_out=sm[:, tb:tb + 1]), r2, t_rs, *pfree[h % 3])
                put(b, x)
                info[h] = (P, sm, x)
            if 1 <= h < 5:
                p = h - 1
                P, sm, x = info[p]
                r3 = V(lambda e, sm=sm: e.reciprocal(sm, sm), x)
                for tb in range(2):
                    r4 = V(lambda e, tb=tb, P=P, sm=sm: e.tensor_scalar(
                        P[:, tb * 256:tb * 256 + 256], P[:, tb * 256:tb * 256 + 256], sm[:, tb:tb + 1], None,
                        ALU.mult), r3)
                info[p] = (P, r4)
            if 2 <= h < 6:
                p = h - 2
                P, tP = info[p]
                b, ps, tf = bank()
                for mb in range(2):
                    for tb in range(2):
                        m = PE(lambda e, mb=mb, tb=tb, P=P, ps=ps: e.transpose(
                            ps[:, mb * 256 + tb * 128:mb * 256 + tb * 128 + 128],
                            P[:, tb * 256 + mb * 128:tb * 256 + mb * 128 + 128], ident[:, :]), tP, *tf)
                PT = attT[p % 2]
                t = V(lambda e, PT=PT, ps=ps: e.tensor_copy(PT, ps[:, :]), m, *tfree[p % 2])
                put(b, t)
                pfree[p % 3] = (m,)
                info[p] = (PT, t)
            if h >= 3:
                p = h - 3
                PT, tP = info[p]
                b, ps, tf = bank()
                for dc in range(2):
                    for mb in range(2):
                        m = PE(lambda e, p=p, dc=dc, mb=mb, PT=PT, ps=ps: e.matmul(
                            ps[:, dc * 256:dc * 256 + 256], VX[:, mb, p * 256 + dc * 128:p * 256 + dc * 128 + 128],
                            PT[:, mb * 256:mb * 256 + 256], start=(mb == 0), stop=(mb == 1)), tP, *t_vx, *tf)
                tfree[p % 2] = (m,)
                t = parts(oT, slice(2 * p, 2 * p + 2), ps[:, :].rearrange("p (a b) -> p a b", a=2), m)
                put(b, t)
                t_o.append(t)
        mx_last = m
        t_h2 = []
        run(layer_tm("xo", 0, oT, Chunks(t_o), ev_res(0, [], t_h2)))
        t_xt = into_next(layer_tm("xo", 1, oT, Chunks(t_o), ev_res(1, [], t_h2)), gains[:, 3, :], t_h2)
        debug("h2", X[:, :, :], *t_h2)

        cols_h = norm_cols(X, junk, t_h2, [mx_last])
        cols_p = cols_h
        if ORDER is not None:
            stop_at[0] = 2 * [n for n, k in ORDER].index("gq") - 1
        XG = Bf[0][:, :].rearrange("p (a d) -> p a d", a=2)
        t_xg, t_gfin = [], []
        acc = []
        for tb in range(2):
            for hf in range(2):
                acc.append(bank())
        qhT = Bf[1][:, 0:512].rearrange("p (c t) -> p c t", c=2)
        sc = [Bf[2][:, 512 * j:512 * j + 512].rearrange("p (a c n) -> p a c n", a=2, c=2) for j in range(2)]
        sc2 = Bf[2][:, 1024:1280].rearrange("p (c n) -> p c n", c=2)
        vt = Bf[1][:, 1536:1568].rearrange("p (c n) -> p c n", c=2)
        it = sb("it", [128, 2, 16], U32)
        itf = Bf[1][:, 1600:1632].rearrange("p (c n) -> p c n", c=2)
        cand = Bf[1][:, 512:768]
        cand2 = Bf[1][:, 768:1024]
        ts = Bf[1][:, 1664:1680]
        pos = sb("pos", [128, 16], U32)
        pi = sb("pi", [128, 2, 16], U32)
        pf = Bf[1][:, 1696:1728].rearrange("p (c n) -> p c n", c=2)
        eq = [Bf[1][:, 1024 + j * 256:1280 + j * 256].rearrange("p (k n) -> p k n", n=16) for j in range(2)]
        si = Bf[1][:, 1760:1792].rearrange("p (c n) -> p c n", c=2)
        ei = Bf[1][:, 1824:1840]
        smx = Bf[1][:, 1856:1858]
        t_idx, t_gw, t_sc = {}, {}, {}
        qh_free, chain = [list(t_h1)], [t_h2[-1]]
        sc_free = [list(t_h2), list(t_h2)]

        def top16(src, work, vals, idx, *toks):
            a = V(lambda e: e.max(out=vals[:, 0:8], in_=src), *toks)
            yield
            V(lambda e: e.max_index(out=idx[:, 0:8], in_max=vals[:, 0:8], in_values=src), a)
            yield
            c = V(lambda e: e.match_replace(out=work, in_to_replace=vals[:, 0:8], in_values=src, imm_value=-3.0e38), a)
            yield
            d = V(lambda e: e.max(out=vals[:, 8:16], in_=work), c)
            yield
            chain[0] = V(lambda e: e.max_index(out=idx[:, 8:16], in_max=vals[:, 8:16], in_values=work), d)
            yield

        def peer_query(h):
            w, n, tw = half("pq", h // 2, h % 2)
            ahead(n + NHL)
            w = [p[:, :].rearrange("p (k n) -> p k n", k=8) for p in w]
            b, ps, tf = bank()
            ts, per = by_chunk(t_xt)
            for c in range(2):
                m = prod(ps[:, c * 256:c * 256 + 256], lambda a, k, c=c: w[a][:, k, c * 128:c * 128 + 128],
                         lambda b_, k: XT[b_][:, k, :], range(8), True, True, tw, *ts, *tf, per=per)
            done(n, m)
            tq = S(lambda e: e.activation(qhT, ps[:, :].rearrange("p (a b) -> p a b", a=2), ACT.Copy), m, *qh_free[0])
            put(b, tq)
            return tq

        def peer_scores(h, tq):
            b, ps, tf = bank()
            for tb in range(2):
                for c in range(2):
                    m = PE(lambda e, c=c, tb=tb, ps=ps: e.matmul(
                        ps[:, (2 * tb + c) * 128:(2 * tb + c) * 128 + 128], qhT[:, c, tb * 128:tb * 128 + 128],
                        skT[:, c, :], start=True, stop=True), tq, t_sk, *tf)
            for tb in range(2):
                t_sc[h] = S(lambda e, ps=ps, tb=tb, r=cols_p[tb][0]: e.activation(
                    sc[h % 2][:, tb, :, :], ps[:, tb * 256:tb * 256 + 256].rearrange("p (c n) -> p c n", c=2),
                    ACT.Copy, scale=r), m, cols_p[tb][1], *sc_free[h % 2])
            put(b, t_sc[h])
            qh_free[0] = [m]

        def peer_topk(h, tb):
            for c in range(2):
                yield from top16(sc[h % 2][:, tb, c, :], sc2[:, c, :], vt[:, c, :], it[:, c, :], t_sc[h], chain[0])
            if tb == 1:
                sc_free[h % 2] = [chain[0]]
            t0 = V(lambda e: e.tensor_copy(itf, it[:, :, :]), chain[0])
            yield
            t1 = V(lambda e: e.tensor_tensor(
                cand.rearrange("p (a b) -> p a b", a=16), vt[:, 0, :].unsqueeze(2).to_broadcast([128, 16, 16]),
                vt[:, 1, :].unsqueeze(1).to_broadcast([128, 16, 16]), ALU.add), chain[0])
            yield
            yield from top16(cand, cand2, ts, pos, t1)
            t2 = chain[0]
            a = V(lambda e: e.tensor_scalar(pi[:, 0, :], pos[:, :], 4, None, ALU.logical_shift_right), t2)
            yield
            b = V(lambda e: e.tensor_scalar(pi[:, 1, :], pos[:, :], 15, None, ALU.bitwise_and), t2)
            yield
            c = V(lambda e: e.tensor_copy(pf, pi[:, :, :]), a, b)
            yield
            for z in range(2):
                d = V(lambda e, z=z: e.tensor_tensor(eq[z], iot[:, :].unsqueeze(1).to_broadcast([128, 16, 16]),
                                                     pf[:, z, :].unsqueeze(2).to_broadcast([128, 16, 16]),
                                                     ALU.is_equal), c, g_i16)
                yield
                f = V(lambda e, z=z: e.tensor_tensor(eq[z], eq[z], itf[:, z, :].unsqueeze(1).to_broadcast([128, 16, 16]),
                                                     ALU.mult), d, t0)
                yield
                f = V(lambda e, z=z: e.tensor_reduce(si[:, z, :], eq[z], AX, ALU.add), f)
                yield
            g = V(lambda e: e.scalar_tensor_tensor(ei, si[:, 0, :], 128.0, si[:, 1, :], ALU.mult, ALU.add), f)
            yield
            t_idx[(h, tb)] = V(lambda e: e.tensor_copy(eidx[:, tb, 16 * h:16 * h + 16], ei), g)
            yield
            gj = gw[:, tb, 16 * h:16 * h + 16]
            a = V(lambda e: e.tensor_scalar(gj, ts, ts[:, 0:1], None, ALU.subtract), t2)
            yield
            x = S(lambda e: e.activation(gj, gj, ACT.Exp, accum_out=smx[:, 0:1]), a)
            a = V(lambda e: e.reciprocal(smx[:, 1:2], smx[:, 0:1]), x)
            yield
            chain[0] = t_gw[(h, tb)] = V(lambda e: e.tensor_scalar(gj, gj, smx[:, 1:2], None, ALU.mult), a)
            yield

        dg2, dg2_free, dgn = diags, dfree, dturn
        t_peer = [None, None]
        NG = 8
        rows = [Bf[j] for j in (6, 7, 8, 9, 10, 3, 4, 5)]
        rows_free = [(mx_last, cols_h[0][1], cols_h[1][1])] * NG
        gn, t_gath = [0], []

        def peer_experts(h, tb):
            for s in range(16 * h, 16 * h + 16, 2):
                dots = []
                for z in range(2):
                    i = gn[0] % NG
                    gn[0] += 1
                    R = rows[i]
                    tg = G.dma(gsem[i], lambda e, z=z, s=s, R=R: e.indirect_dma_start(
                        out=R[:, :], out_offset=None, in_=A["ex"],
                        in_offset=bass.IndirectOffsetOnAxis(ap=eidx[:, tb, s + z:s + z + 1], axis=0)),
                        t_idx[(h, tb)], g_last, *rows_free[i])
                    d = V(lambda e, z=z, s=s, R=R: e.tensor_tensor_reduce(
                        R[:, 0:1024], R[:, 0:1024], XG[:, tb, :], 1.0, 0.0, ALU.mult, ALU.add,
                        av_[:, tb, s + z:s + z + 1]), tg, t_xg[tb])
                    t_gath.append(tg)
                    dots.append((i, R, tg, d))
                a = S(lambda e, s=s: e.activation(av_[:, tb, s:s + 2], av_[:, tb, s:s + 2], ACT.Gelu), dots[0][3],
                      dots[1][3])
                b = V(lambda e, s=s: e.tensor_tensor(av_[:, tb, s:s + 2], av_[:, tb, s:s + 2], gw[:, tb, s:s + 2],
                                                     ALU.mult), a, t_gw[(h, tb)])
                for z, (i, R, tg, d) in enumerate(dots):
                    n = dgn[0] % 4
                    dgn[0] += 1
                    c = S(lambda e, n=n, s=s, z=z: e.activation(dg2[:, n, :], ident[:, :], ACT.Copy,
                                                                scale=av_[:, tb, s + z:s + z + 1]), b, *dg2_free[n])
                    for hf in range(2):
                        bi, ps, tf = acc[2 * tb + hf]
                        m = PE(lambda e, n=n, hf=hf, ps=ps, R=R, f=(s + z == 0), l=(s + z == 127): e.matmul(
                            ps[:, :], dg2[:, n, :], R[:, 1024 + 512 * hf:1536 + 512 * hf], start=f, stop=l),
                            c, tg, *tf)
                    dg2_free[n] = (m,)
                    rows_free[i] = (m, d)
                yield
            t_peer[tb] = m

        eager[0] = False
        peer_scores(0, peer_query(0))
        run(peer_topk(0, 0))
        for tb in range(2):
            c, tc = cols_h[tb]
            t_xg.append(V(lambda e, tb=tb, c=c: e.scalar_tensor_tensor(XG[:, tb, :], X[:, tb, :], c, GB[:, :], ALU.mult,
                                                                       ALU.mult), tc, t_gffn, *t_h2, *t_h1))
        t_gfin = S.dma([sem("c_gfin"), 0], lambda e: e.dma_start(GB[:, :], A["gfin"].partition_broadcast(128)), *t_xg)
        debug("eidx", eidx[:, 0, 0:16], *t_idx.values())
        for h in range(8):
            for tb in range(2):
                nxt = iter(())
                if (h, tb) != (7, 1):
                    nxt = peer_topk(h + tb, 1 - tb)
                for n, _ in enumerate(peer_experts(h, tb)):
                    for _ in range(5):
                        next(nxt, None)
                    if tb == 0 and h < 7 and n == 1:
                        tq = peer_query(h + 1)
                    if tb == 0 and h < 7 and n == 3:
                        peer_scores(h + 1, tq)
                run(nxt)
        t_h3 = []
        for tb in range(2):
            for hf in range(2):
                bi, ps, _ = acc[2 * tb + hf]
                t = V(lambda e, tb=tb, hf=hf, ps=ps: e.tensor_tensor(X[:, tb, hf * 512:hf * 512 + 512], ps[:, :],
                                                                     X[:, tb, hf * 512:hf * 512 + 512], ALU.add),
                      t_peer[tb], *t_xg)
                put(bi, t)
                t_h3.append(t)
        debug("h3", X[:, :, :], *t_h3)

        stop_at[0] = 1 << 20
        after.append(t_gath[-3])
        eager[0] = True
        preload()
        cr1, cr2, cr3 = col(2), col(2), col(2)
        a1 = S(lambda e: e.activation(junk[:, 0, :], X[:, 0, :], ACT.Square, accum_out=cr1[:, 0:1]), *t_h3)
        a2 = S(lambda e: e.activation(junk[:, 1, :], X[:, 1, :], ACT.Square, accum_out=cr1[:, 1:2]), *t_h3)
        HG = Bf[8][:, :].rearrange("p (a d) -> p a d", a=2)
        b1 = V(lambda e: e.tensor_tensor(HG, X[:, :, :], GB[:, :].unsqueeze(1).to_broadcast([128, 2, 1024]), ALU.mult),
               t_gfin, *t_h3)
        a3 = S(lambda e: e.activation(junk[:, 0, :], HG[:, 0, :], ACT.Square, accum_out=cr2[:, 0:1]), b1, a1)
        b2 = V(lambda e: e.tensor_tensor_reduce(junk[:, 1, :], HG[:, 1, :], HG[:, 1, :], 1.0, 0.0, ALU.mult, ALU.add,
                                                cr2[:, 1:2]), b1, a2)
        vv, rr, qq = col(4), col(4), col(4)
        t = V(lambda e: e.tensor_scalar(vv[:, 0:2], cr1, 1.0 / 1024, EPS, ALU.mult, ALU.add), a1, a2)
        t = V(lambda e: e.reciprocal(rr[:, 0:2], vv[:, 0:2]), t)
        t = V(lambda e: e.tensor_tensor(vv[:, 2:4], cr2, rr[:, 0:2], ALU.mult), t, a3, b2)
        t = V(lambda e: e.tensor_scalar(vv[:, 2:4], vv[:, 2:4], 1.0 / 1024, EPS, ALU.mult, ALU.add), t)
        t = S(lambda e: e.activation(rr, vv, ACT.Sqrt), t)
        t = V(lambda e: e.reciprocal(rr, rr), t)
        t = V(lambda e: e.tensor_tensor(qq, vv, rr, ALU.mult), t)
        t = V(lambda e: e.tensor_tensor(qq, qq, rr, ALU.mult), t)
        t = V(lambda e: e.tensor_scalar(qq, qq, -0.5, 1.5, ALU.mult, ALU.add), t)
        t_r1 = V(lambda e: e.tensor_tensor(rr, rr, qq, ALU.mult), t)
        b3 = V(lambda e: e.tensor_tensor(cr3, rr[:, 0:2], rr[:, 2:4], ALU.mult), t_r1)
        t_ggn = S.dma([sem("c_ggn"), 0], lambda e: e.dma_start(GB[:, :], A["ggn"].partition_broadcast(128)), b1)
        eager[0] = False
        t_xt = transposed(HG, [(cr3[:, 0:1], b3), (cr3[:, 1:2], b3)], gains[:, 4, :], XT, [b1], [])
        eager[0] = True
        ahead(used[0] + 2)
        t_x2 = [V(lambda e, tb=tb: e.tensor_scalar(X[:, tb, :], HG[:, tb, :], rr[:, tb:tb + 1], None, ALU.mult),
                  a2, t_r1) for tb in range(2)]
        debug("x2", X[:, :, :], *t_x2)
        scanm = Bf[9][:, 0:1024]
        gw2 = Bf[9][0:16, 1024:1536]
        glr = Bf[9][0:16, 1536:1792]
        g_s0 = G(lambda e: e.memset(scanm, 1.0), b3)
        g_scan = G(lambda e: e.memset(scanm.rearrange("p (a b) -> p a b", b=64)[:, :, 0:1], 0.0), g_s0)
        t_gw2 = S.dma([sem("c_gw2"), 0], lambda e: e.dma_start(gw2, A["gw2"]), b3)

        v4_ = lambda ap: ap.rearrange("p (h t) -> p h t", h=4)
        zb, lfb = Bf[0][:, 0:1024], Bf[0][:, 1024:2048]
        et, klT = Bf[1][:, 0:1024], Bf[1][:, 1024:2048]
        qd, kd = Bf[2][:, 0:1024], Bf[2][:, 1024:2048]
        kk_, klt = Bf[3][:, 0:1024], Bf[3][:, 1024:2048]
        b, ps, tf = bank()
        m = prod(ps[0:16, 0:256], lambda a, k: thinr[a][:, k, 8:24], lambda b_, k: XT[b_][:, k, :], range(8), True,
                 True, t_th, *t_xt, *tf)
        t = S(lambda e, ps=ps: e.activation(glr, ps[0:16, 0:256], ACT.Copy), m)
        put(b, t)
        tz = []
        for hp in range(2):
            b, ps, tf = bank()
            for c in range(2):
                h = 2 * hp + c
                m = PE(lambda e, c=c, h=h, ps=ps: e.matmul(ps[:, c * 256:c * 256 + 256], gw2[:, h * 128:h * 128 + 128],
                                                           glr, start=True, stop=True), t, t_gw2, *tf)
            for c in range(2):
                h = 2 * hp + c
                tt = S(lambda e, c=c, h=h, ps=ps: e.activation(zb[:, h * 256:h * 256 + 256],
                                                               ps[:, c * 256:c * 256 + 256], ACT.Identity,
                                                               bias=gb2[:, h:h + 1]), m, t_gb2, *t_h3)
                tz.append(tt)
            put(b, tt)
        a = S(lambda e: e.activation(lfb, zb, ACT.Abs), *tz)
        x = S(lambda e: e.activation(lfb, lfb, ACT.Exp, scale=-1.0), a)
        x = S(lambda e: e.activation(lfb, lfb, ACT.Ln, bias=1.0), x)
        a = V(lambda e: e.scalar_tensor_tensor(zb, zb, 0.0, lfb, ALU.min, ALU.subtract), x)
        tb_ = V(lambda e: e.tensor_tensor_scan(lfb, scanm, zb, 0.0, ALU.mult, ALU.add), a, g_scan)
        x1 = S(lambda e: e.activation(et, lfb, ACT.Exp, scale=0.0625), tb_, *t_h3)
        dec = small[:, 16:32]
        l16 = lfb.rearrange("p (c n) -> p c n", n=64)
        t_dec = S(lambda e: e.activation(dec, l16[:, :, 63], ACT.Exp, scale=0.0625), tb_)
        t_qd, t_k = [], []
        run(layer_fm("gq", 0, XT, t_xt, lambda hf, ps, m: V(lambda e: e.scalar_tensor_tensor(
            qd[:, hf * 512:hf * 512 + 512], ps.rearrange("p a b -> p (a b)"), 128.0 ** -0.5,
            et[:, hf * 512:hf * 512 + 512], ALU.mult, ALU.mult), m, x1), t_qd))
        run(layer_fm("gk", 0, XT, t_xt, lambda hf, ps, m: S(lambda e: e.activation(
            kk_[:, hf * 512:hf * 512 + 512], ps.rearrange("p a b -> p (a b)"), ACT.Copy), m), t_k))
        x2 = S(lambda e: e.activation(et, lfb, ACT.Exp, scale=-0.0625), tb_, *t_qd)
        t_kd = V(lambda e: e.tensor_tensor(kd, kk_, et, ALU.mult), x2, *t_k)
        a = V(lambda e: e.tensor_tensor(zb.rearrange("p (c n) -> p c n", n=64),
                                        l16[:, :, 63:64].to_broadcast([128, 16, 64]), l16, ALU.subtract), tb_)
        x3 = S(lambda e: e.activation(zb, zb, ACT.Exp, scale=0.0625), a)
        t_kl = V(lambda e: e.tensor_tensor(klT, kk_, zb, ALU.mult), x3, *t_k)
        gv = Bf[4][:, :].rearrange("p (a d) -> p a d", a=2)
        t_gv = []
        for k in range(2):
            run(layer_tm("gv", k, XT, t_xt, lambda tb, ps, m, k=k: S(
                lambda e: e.activation(gv[:, tb, k * 512:k * 512 + 512], ps[:, :], ACT.Copy), m, *t_h3), t_gv))
        gr = Bf[6][:, :].rearrange("p (a d) -> p a d", a=2)
        t_gr = []

        def ev_gr(k):
            def ev(tb, ps, m):
                t = S(lambda e: e.activation(gr[:, tb, k * 512:k * 512 + 512], ps[:, :], ACT.Silu), m, *t_h3)
                t_gr.append(V(lambda e: e.tensor_tensor(gr[:, tb, k * 512:k * 512 + 512],
                                                        gr[:, tb, k * 512:k * 512 + 512],
                                                        GB[:, k * 512:k * 512 + 512], ALU.mult), t, t_ggn))
                return t
            return ev

        BQ = Bf[8][:, :].rearrange("p (k t) -> p k t", k=8)
        BK = Bf[9][:, :].rearrange("p (k t) -> p k t", k=8)
        BV = Bf[3][:, :].rearrange("p (a d) -> p a d", a=2)
        sq = Bf[10][:, :].rearrange("p (j n) -> p j n", j=4)
        xdiag = Bf[1][:, 1536:2048].rearrange("p (j n) -> p j n", j=4)
        xfree = [[]] * 4
        sqf = [[tb_, m], [tb_, m], [tb_, m], [tb_, m]]
        t_bn = {"bq": [], "bk": []}
        b_old = [tb_, m, *t_x2]

        def bn_layer(name, k, dst, gcol):
            ss = col(8)
            done_, sqs = [], []

            def ev(hf, ps, m):
                c = 4 * k + 2 * hf
                j = (2 * k + hf) % 4
                t = S(lambda e: e.activation(dst[:, c:c + 2, :], ps, ACT.Copy), m, *b_old)
                done_.append(t)
                sqs.append((j, S(lambda e: e.activation(sq[:, j, :], dst[:, c:c + 2, :].rearrange("p a b -> p (a b)"),
                                                        ACT.Square), t, *sqf[j])))
                return t

            tr = []

            def stats():
                b, psn, tf = bank()
                for c in range(4):
                    j, tq = sqs[c // 2]
                    for tb in range(2):
                        o = (c % 2) * 256 + tb * 128
                        m = PE(lambda e, c=c, tb=tb, o=o, j=j: e.matmul(psn[:, 2 * c + tb:2 * c + tb + 1], sq[:, j, o:o + 128],
                                                                        ones[:, 0:1], start=True, stop=True), tq, g_on, *tf)
                    sqf[j] = [m]
                t = V(lambda e: e.tensor_copy(ss, psn[:, 0:8]), m)
                put(b, t)
                t = rstd(ss, 128, t)
                for q in range(8):
                    dg, fr, j = (diags[:, q, :], dfree, q) if q < 4 else (xdiag[:, q - 4, :], xfree, q - 4)
                    r = ss[:, q:q + 1]
                    if q % 2:
                        d = V(lambda e, dg=dg, r=r: e.tensor_scalar(dg, ident[:, :], r, None, ALU.mult), t, *fr[j])
                    else:
                        d = S(lambda e, dg=dg, r=r: e.activation(dg, ident[:, :], ACT.Copy, scale=r), t, *fr[j])
                    tr.append((dg, d, fr, j))
                return iter(())

            def spread():
                for hp in range(2):
                    b, ps, tf = bank()
                    for c in range(2):
                        for tb in range(2):
                            dg, d, fr, j = tr[4 * hp + 2 * c + tb]
                            m = PE(lambda e, c=c, tb=tb, dg=dg, ps=ps: e.matmul(
                                ps[:, c * 256 + tb * 128:c * 256 + tb * 128 + 128], ones[:, :], dg, start=True,
                                stop=True), d, g_on, *tf)
                            fr[j] = (m,)
                    f = dst[:, 4 * k + 2 * hp:4 * k + 2 * hp + 2, :].rearrange("p a b -> p (a b)")
                    t = V(lambda e, f=f, ps=ps: e.scalar_tensor_tensor(f, f, gcol, ps[:, :], ALU.mult, ALU.mult), m,
                          t_bqk, *done_)
                    put(b, t)
                    t_bn[name].append(t)
                return iter(())

            return lambda: layer_fm(name, k, XT, t_xt, ev), stats, spread

        t_bv = []
        q0, q1, k0, k1 = (bn_layer(n, k, d, bqk[:, z:z + 1]) for n, d, z in (("bq", BQ, 0), ("bk", BK, 1))
                          for k in range(2))
        r0, r1 = (lambda k=k: layer_tm("gr", k, XT, t_xt, ev_gr(k)) for k in range(2))
        v0, v1 = (lambda k=k: layer_tm("bv", k, XT, t_xt, lambda tb, ps, m: S(
            lambda e: e.activation(BV[:, tb, k * 512:k * 512 + 512], ps[:, :], ACT.Copy), m, *t_S.values()), t_bv)
            for k in range(2))
        fills.extend([r0, q0[0], r1, q0[1], q1[0], q0[2], k0[0], q1[1], v0, q1[2], k0[1], k1[0], k0[2], k1[1], v1,
                      k1[2]])
        fill(2)
        AT = Bf[0][:, 0:512]
        t_at0 = V(lambda e: e.memset(AT, 0.0), x3, t_kl)
        b, ps, tf = bank()
        for h in range(4):
            for n in range(4):
                o = 64 * (n % 2)
                m = PE(lambda e, h=h, n=n, o=o, ps=ps: e.matmul(
                    ps[o:o + 64, (h * 2 + n // 2) * 64:(h * 2 + n // 2) * 64 + 64],
                    kd[:, h * 256 + n * 64:h * 256 + n * 64 + 64], qd[:, h * 256 + n * 64:h * 256 + n * 64 + 64],
                    start=True, stop=True), t_kd, *t_qd, *tf)
        t_at = V(lambda e, ps=ps: e.copy_predicated(AT.rearrange("p (a b) -> p a b", b=64),
                                                    cmask[:, :].bitcast(I32).unsqueeze(1).to_broadcast([128, 8, 64]),
                                                    ps[:, :].rearrange("p (a b) -> p a b", b=64)), m, t_at0, g_cm)
        put(b, t_at)
        fill()
        t_klt = []
        for tb in range(2):
            b, ps, tf = bank()
            for h in range(4):
                m = PE(lambda e, tb=tb, h=h, ps=ps: e.transpose(
                    ps[:, h * 128:h * 128 + 128], klT[:, h * 256 + tb * 128:h * 256 + tb * 128 + 128], ident[:, :]),
                    t_kl, *tf)
            t = S(lambda e, tb=tb, ps=ps: e.activation(klt[:, tb * 512:tb * 512 + 512], ps[:, :], ACT.Copy), m)
            put(b, t)
            t_klt.append(t)
        xfree[:] = [tuple(t_klt)] * 4
        SA = [Bf[5][:, 0:1024], Bf[5][:, 1024:2048], Bf[1][:, 0:1024]]
        t_S = {}
        for n in range(3):
            for hp in range(2):
                b, ps, tf = bank()
                o = 64 * (n % 2)
                for c in range(2):
                    h = 2 * hp + c
                    m = PE(lambda e, c=c, h=h, n=n, o=o, ps=ps: e.matmul(
                        ps[:, c * 256:c * 256 + 256],
                        klt[o:o + 64, (n // 2) * 512 + h * 128:(n // 2) * 512 + h * 128 + 128],
                        gv[o:o + 64, n // 2, h * 256:h * 256 + 256], start=True, stop=True), *t_klt, *t_gv, *tf)
                if n == 0:
                    t = V(lambda e, hp=hp, ps=ps: e.tensor_copy(SA[0][:, hp * 512:hp * 512 + 512], ps[:, :]), m)
                else:
                    for c in range(2):
                        h = 2 * hp + c
                        t = V(lambda e, c=c, h=h, n=n, ps=ps: e.scalar_tensor_tensor(
                            SA[n][:, h * 256:h * 256 + 256], SA[n - 1][:, h * 256:h * 256 + 256],
                            dec[:, h * 4 + n:h * 4 + n + 1], ps[:, c * 256:c * 256 + 256], ALU.mult, ALU.add),
                            m, t_dec, t_S[(n - 1, hp)], t_kd)
                put(b, t)
                t_S[(n, hp)] = t
            fill()
        assert len(t_gr) == 4
        oN = Bf[7][:, :].rearrange("p (a d) -> p a d", a=2)
        t_on = []
        for tb in range(2):
            for hp in range(2):
                b, ps, tf = bank()
                for c in range(2):
                    h = 2 * hp + c
                    for q in range(2):
                        n = 2 * tb + q
                        o = 64 * q
                        m = PE(lambda e, c=c, h=h, n=n, o=o, ps=ps, tb=tb: e.matmul(
                            ps[o:o + 64, c * 256:c * 256 + 256], AT[o:o + 64, (h * 2 + tb) * 64:(h * 2 + tb) * 64 + 64],
                            gv[o:o + 64, tb, h * 256:h * 256 + 256], start=True, stop=(n == 0)), t_at, *t_gv, *tf)
                        if n:
                            m = PE(lambda e, c=c, h=h, n=n, o=o, ps=ps: e.matmul(
                                ps[o:o + 64, c * 256:c * 256 + 256], qd[:, h * 256 + n * 64:h * 256 + n * 64 + 64],
                                SA[n - 1][:, h * 256:h * 256 + 256], start=False, stop=True), t_S[(n - 1, hp)])
                ss = col(2)
                for c in range(2):
                    x = S(lambda e, c=c, ss=ss, ps=ps: e.activation(klT[:, c * 256:c * 256 + 256],
                                                                    ps[:, c * 256:c * 256 + 256], ACT.Square,
                                                                    accum_out=ss[:, c:c + 1]), m, *t_klt)
                r = rstd(ss, 256, x)
                for c in range(2):
                    h = 2 * hp + c
                    t = V(lambda e, c=c, h=h, tb=tb, ss=ss, ps=ps: e.scalar_tensor_tensor(
                        oN[:, tb, h * 256:h * 256 + 256], ps[:, c * 256:c * 256 + 256], ss[:, c:c + 1],
                        gr[:, tb, h * 256:h * 256 + 256], ALU.mult, ALU.mult), r, *t_gr, *t_h3)
                put(b, t)
                t_on.append(t)
        debug("oN", oN, *t_on)
        t_gla_last = m

        fill(99)
        oT2 = [Br[j][:, :].rearrange("p (k t) -> p k t", k=8) for j in (0, 10)]
        t_oT = transposed(oN, None, None, oT2, t_on, [t_gla_last])
        SGA = Bf[4][:, :].rearrange("p (k t) -> p k t", k=8)
        SGB = Bf[6][:, :].rearrange("p (k t) -> p k t", k=8)
        yT = Bf[5][:, :].rearrange("p (k t) -> p k t", k=8)
        t_ga, t_gb, t_ya = [], [], []
        for k in range(2):
            fills.append(lambda k=k: layer_fm("ga", k, XT, t_xt, lambda hf, ps, m: S(
                lambda e: e.activation(SGA[:, 4 * k + 2 * hf:4 * k + 2 * hf + 2, :], ps, ACT.Sigmoid), m,
                t_gla_last), t_ga))
            fills.append(lambda k=k: layer_fm("gb", k, XT, t_xt, lambda hf, ps, m: S(
                lambda e: e.activation(SGB[:, 4 * k + 2 * hf:4 * k + 2 * hf + 2, :], ps, ACT.Sigmoid), m, *t_on),
                t_gb))
        for k in range(2):
            fills.append(lambda k=k: layer_fm("wa", k, oT2, t_oT, lambda hf, ps, m: V(
                lambda e: e.tensor_tensor(yT[:, 4 * k + 2 * hf:4 * k + 2 * hf + 2, :], ps,
                                          SGA[:, 4 * k + 2 * hf:4 * k + 2 * hf + 2, :], ALU.mult), m, *t_ga,
                t_gla_last), t_ya))
        mT_ = [Br[j][:, :].rearrange("p (k t) -> p k t", k=8) for j in (7, 1)]
        attP = [Bf[2][:, 384 * j:384 * j + 384] for j in range(3)]
        attT = [Bf[2][:, 1152 + 384 * j:1536 + 384 * j] for j in range(2)]
        bia = [diags[:, 2 * j:2 * j + 2, :].rearrange("p a b -> p (a b)") for j in range(2)]
        pfree = [[t_gla_last]] * 3
        tfree = [[t_gla_last]] * 2
        bfree = [dfree[0] + dfree[1] + dfree[2] + dfree[3]] * 2
        SC = 128.0 ** -0.5
        t_m = []
        for h in range(11):
            if h < 8:
                bh = bia[h % 2]
                slope = 2.0 ** (-(h + 1))
                tbi = V(lambda e, bh=bh, slope=slope: e.tensor_scalar(bh, DD[:, :], slope / SC, None, ALU.mult), g_dd,
                        *bfree[h % 2])
                b, psS, tf = bank()
                PE(lambda e, psS=psS, h=h: e.matmul(psS[:, 0:128], BQ[:, h, 0:128], BK[:, h, 0:128], start=True,
                                                    stop=True), *t_bn["bq"], *t_bn["bk"], *tf)
                mS = PE(lambda e, psS=psS, h=h: e.matmul(psS[:, 128:384], BQ[:, h, 128:256], BK[:, h, :], start=True,
                                                         stop=True), *t_bn["bq"], *t_bn["bk"], *tf)
                P = attP[h % 3]
                mx, sm = col(2), col(2)
                V(lambda e, P=P, psS=psS, mx=mx, bh=bh: e.tensor_tensor_reduce(
                    P[:, 0:128], psS[:, 0:128], bh[:, 128:256], SC, NEG, ALU.add, ALU.max, mx[:, 0:1]), mS, tbi,
                    *pfree[h % 3])
                r2 = V(lambda e, P=P, psS=psS, mx=mx, bh=bh: e.tensor_tensor_reduce(
                    P[:, 128:384], psS[:, 128:384], bh, SC, NEG, ALU.add, ALU.max, mx[:, 1:2]), mS, tbi,
                    *pfree[h % 3])
                put(b, r2)
                bfree[h % 2] = [r2]
                r3 = V(lambda e, mx=mx: e.tensor_scalar(mx, mx, -1.0, None, ALU.mult), r2)
                for tb, (c0, c1) in enumerate(((0, 128), (128, 384))):
                    x1 = S(lambda e, P=P, c0=c0, c1=c1, tb=tb, mx=mx, sm=sm: e.activation(
                        P[:, c0:c1], P[:, c0:c1], ACT.Exp, bias=mx[:, tb:tb + 1], accum_out=sm[:, tb:tb + 1]), r3)
                info[h] = (P, sm, x1)
            if 1 <= h < 9:
                p = h - 1
                P, sm, x1 = info[p]
                r5 = V(lambda e, sm=sm: e.reciprocal(sm, sm), x1)
                V(lambda e, P=P, sm=sm: e.tensor_scalar(P[:, 0:128], P[:, 0:128], sm[:, 0:1], None, ALU.mult), r5)
                r6 = V(lambda e, P=P, sm=sm: e.tensor_scalar(P[:, 128:384], P[:, 128:384], sm[:, 1:2], None, ALU.mult),
                       r5)
                info[p] = (P, r6)
            late_splits()
            fill_late()
            if 2 <= h < 10:
                p = h - 2
                P, tP = info[p]
                b, psT, tf = bank()
                for j in range(3):
                    mT = PE(lambda e, j=j, P=P, psT=psT: e.transpose(psT[:, j * 128:j * 128 + 128],
                                                                     P[:, j * 128:j * 128 + 128], ident[:, :]),
                            tP, *tf)
                PT = attT[p % 2]
                t = S(lambda e, PT=PT, psT=psT: e.activation(PT, psT[:, 0:384], ACT.Copy), mT, *tfree[p % 2])
                put(b, t)
                pfree[p % 3] = (mT,)
                info[p] = (PT, t)
            if h >= 3:
                p = h - 3
                PT, tP = info[p]
                if p % 2 == 0:
                    bV, psV, tfV = bank()
                o = 256 * (p % 2)
                vs = [BV[:, s, p * 128:p * 128 + 128] for s in range(2)]
                PE(lambda e, PT=PT, vs=vs, o=o, psV=psV: e.matmul(psV[:, o:o + 128], vs[0], PT[:, 0:128], start=True,
                                                                  stop=True), tP, *t_bv, *tfV)
                PE(lambda e, PT=PT, vs=vs, o=o, psV=psV: e.matmul(psV[:, o + 128:o + 256], vs[0], PT[:, 128:256],
                                                                  start=True, stop=False), tP)
                mV = PE(lambda e, PT=PT, vs=vs, o=o, psV=psV: e.matmul(psV[:, o + 128:o + 256], vs[1], PT[:, 256:384],
                                                                       start=False, stop=True), tP)
                tfree[p % 2] = (mV,)
                if p % 2 == 1:
                    t = parts(mT_, slice(p - 1, p + 1), psV[:, :].rearrange("p (a b) -> p a b", a=2), mV, *t_oT,
                              *t_bn["bq"], *t_bn["bk"])
                    put(bV, t)
                    t_m.append(t)
        fill(99)
        for j in range(4):
            dfree[j] = tuple(bfree[0]) + tuple(bfree[1])
        t_y = []
        tmp = Bf[8][:, :].rearrange("p (k t) -> p k t", k=8)

        yR = [Br[j][:, :].rearrange("p (k t) -> p k t", k=8) for j in (2, 3)]

        def ev_wb(k):
            def ev(hf, ps, m):
                c = 4 * k + 2 * hf
                t = V(lambda e: e.tensor_tensor(tmp[:, c:c + 2, :], ps, SGB[:, c:c + 2, :], ALU.mult), m, *t_gb, mS)
                a = V(lambda e: e.tensor_tensor(yT[:, c:c + 2, :], yT[:, c:c + 2, :], tmp[:, c:c + 2, :], ALU.add), t,
                      *t_ya)
                t_y.append(parts(yR, slice(c, c + 2), yT[:, c:c + 2, :], a, mV))
                return t
            return ev

        for k in range(2):
            run(layer_fm("wb", k, mT_, Chunks(t_m), ev_wb(k)))
        t_x3 = []
        run(layer_tm("wo2", 0, yR, Chunks(t_y), ev_res(0, t_xt, t_x3)))
        t_xt = into_next(layer_tm("wo2", 1, yR, Chunks(t_y), ev_res(1, t_xt, t_x3)), gains[:, 5, :], t_x3)
        m_w = PE.items[-1][2]
        debug("x3", X[:, :, :], *t_x3)

        junk = Bf[9][:, :].rearrange("p (a d) -> p a d", a=2)
        cols_h = norm_cols(X, junk, t_x3, [mS])
        eager[0] = True
        ahead(used[0] + NHL)
        rsq = col(2)
        t_rsq = V(lambda e, c=cols_h[2]: e.tensor_tensor(rsq, c, c, ALU.mult), cols_h[0][1])
        U = [[Br[j + 4 * z][:, :].rearrange("p (k t) -> p k t", k=8) for z in range(2)] for j in range(4)]
        ufree = [*t_y, mV, m_w, *t_x3]
        t_u = {j: [] for j in range(4)}
        rel = [Bf[8][:, 1024 * j:1024 * j + 512].rearrange("p (a b) -> p a b", a=2) for j in range(2)]
        sqr = [Bf[8][:, 1024 * j + 512:1024 * j + 1024].rearrange("p (a b) -> p a b", a=2) for j in range(2)]
        relf = [list(t_y), list(t_y)]

        def ev_up(k):
            def ev(hf, ps, m):
                c = slice(4 * (k % 2) + 2 * hf, 4 * (k % 2) + 2 * hf + 2)
                u, r, q = U[k // 2], rel[hf], sqr[hf]
                t = S(lambda e: e.activation(r, ps, ACT.Relu), m, *relf[hf])
                a = S(lambda e: e.activation(u[0][:, c, :], r, ACT.Square), t, *ufree)
                b = V(lambda e: e.tensor_tensor(q, r, r, ALU.mult), t, *relf[hf])
                b = V(lambda e: e.tensor_tensor(u[1][:, c, :], q, u[0][:, c, :].bitcast(F32), ALU.subtract), a, b,
                      *ufree)
                relf[hf] = [a, b]
                t_u[k // 2].append(b)
                return t
            return ev

        pT = Bf[10][:, 1024:1536].rearrange("p (k t) -> p k t", k=2)
        pR = [Br[10][:, 512 * z:512 * z + 512].rearrange("p (k t) -> p k t", k=2) for z in range(2)]
        t_p = S.dma([sem("c_pT"), 0], lambda e: e.dma_start(pT, A["pT"]), *t_ya)
        for k in range(8):
            run(layer_fm("up", k, XT, t_xt, ev_up(k)))
            if k == 6:
                t_p = parts(pR, slice(0, 2), pT, t_p, *t_ya)
        t_x4 = []

        def ev_dn(k):
            def ev(tb, ps, m):
                t = V(lambda e: e.scalar_tensor_tensor(X[:, tb, k * 512:k * 512 + 512], ps[:, :], rsq[:, tb:tb + 1],
                                                       X[:, tb, k * 512:k * 512 + 512], ALU.mult, ALU.add), m, t_rsq)
                t_x4.append(t)
                return t
            return ev

        PW = Bf[5][:, :].rearrange("p (a d) -> p a d", a=2)
        t_pw = []

        def ple_product():
            w, n_, tw = half("ple", 0, 0)
            w = [p[:, :].rearrange("p (k n) -> p k n", k=2) for p in w]
            for tb in range(2):
                for hf in range(2):
                    b, ps, tf = bank()
                    m = prod(ps[:, :], lambda a, k, tb=tb: pR[a][:, k, tb * 128:tb * 128 + 128],
                             lambda b_, k, hf=hf, w=w: w[b_][:, k, hf * 512:hf * 512 + 512], range(2), True, True,
                             tw, t_p, *tf)
                    t = S(lambda e, tb=tb, hf=hf, ps=ps: e.activation(PW[:, tb, hf * 512:hf * 512 + 512], ps[:, :],
                                                                      ACT.Copy), m)
                    put(b, t)
                    t_pw.append(t)
            done(n_, m)

        for hf in range(2):
            bk = [bank() for _ in range(2)]
            for r in range(4):
                g_ = layer_tm("dn", 4 * hf + r, U[r], t_u[r], ev_dn(hf), bk=bk, start=(r == 0), stop=(r == 3))
                if hf and r == 3:
                    t_xt = into_next(g_, gains[:, 6, :], t_x4, ple_product)
                else:
                    run(g_)
        debug("x4", X[:, :, :], *t_x4)

        cols_g = norm_cols(X, junk, t_x4, [])
        eager[0] = True
        ahead(used[0] + NHL)
        SG = Bf[6][:, :].rearrange("p (a d) -> p a d", a=2)
        s_out = [sem("s_out"), 0]
        t_out = []

        def ev_pg(k):
            def ev(tb, ps, m):
                c = slice(k * 512, k * 512 + 512)
                t = S(lambda e: e.activation(SG[:, tb, c], ps[:, :], ACT.Sigmoid,
                                              scale=cols_g[tb][0]), m, cols_g[tb][1], *t_x4)
                a = V(lambda e: e.tensor_tensor(SG[:, tb, c], SG[:, tb, c], PW[:, tb, c], ALU.mult), t, *t_pw)
                a = V(lambda e: e.tensor_tensor(SG[:, tb, c], SG[:, tb, c], X[:, tb, c], ALU.add), a)
                t_out.append(SP.dma(s_out, lambda e: e.dma_start(out[tb * 128:tb * 128 + 128, c], SG[:, tb, c]), a))
                return t
            return ev

        for k in range(2):
            run(layer_tm("pg", k, XT, t_xt, ev_pg(k)))
        SP(lambda e: e.nop(), t_out[-1])

        assert used[0] == len(dma_order)
        if ORDER is None:
            print(dma_order)
        for q in (SP, S, V, PE, G):
            q.number()
        block = ctx.enter_context(nc.Block())

        @block.sync
        def _(e):
            SP.emit(e)

        @block.scalar
        def _(e):
            S.emit(e)

        @block.vector
        def _(e):
            V.emit(e)

        @block.tensor
        def _(e):
            PE.emit(e)

        @block.gpsimd
        def _(e):
            G.emit(e)


def layout(inp):
    def halves(w, kind):
        rows, n = w.shape
        out = []
        for c in range(0, n, 512):
            for r in range(0, rows, 1024):
                t = w[r:r + 1024, c:c + 512].reshape(8, 128, -1).transpose(1, 0, 2)
                if t.shape[2] == 256:
                    out.append(t.reshape(128, 2048))
                elif kind == "f":
                    out += [t[:, :, 0:256].reshape(128, 2048), t[:, :, 256:512].reshape(128, 2048)]
                else:
                    out += [t[:, 0:4, :].reshape(128, 2048), t[:, 4:8, :].reshape(128, 2048)]
        return out

    def cols(v, k):
        return np.ascontiguousarray(v.reshape(k, 128).T)

    g = {k: np.asarray(v) for k, v in inp.items()}
    w = g["w_in"][0]
    aq = w[:, 1544:2056].reshape(1024, 8, 64)[:, [0, 4, 1, 5, 2, 6, 3, 7], :].reshape(1024, 512)
    src = {"qk": w[:, 0:512], "aq": aq, "mv": w[:, 512:1024], "mo": w[:, 1024:1536], "wo1": g["w_out"][0],
           "xq": g["w_xq"][0], "xk": g["w_xk"][0], "xv": g["w_xv"][0], "xo": g["w_xo"][0], "pq": g["w_pq"][0]}
    v = g["w_in_2"][0]
    at = 0
    for name, n in (("gq", 512), ("gk", 512), ("gv", 1024), ("lr", 16), ("gr", 1024), ("bq", 1024), ("bk", 1024),
                    ("bv", 1024), ("ga", 1024), ("gb", 1024)):
        src[name] = v[:, at:at + n]
        at += n
    src |= {"wa": g["w_branch_a_2"][0], "wb": g["w_branch_b_2"][0], "wo2": g["w_out_2"][0], "up": g["w_up_2"][0],
            "dn": g["w_down_2"][0], "pg": g["w_ple_gate_2"][0]}
    src["akv"] = w[:, 2056:2312]
    wt = np.stack([t for name, _, kind in TILES for t in halves(src[name], kind)])
    thin = np.concatenate([w[:, 1536:1544], src["lr"]], axis=1)
    return {
        "x": g["x"][0], "mem": g["mem"][0], "wt": wt,
        "gains": np.stack([cols(g[n].reshape(-1), 8) for n in ("g_mix", "g_mem", "g_cross", "g_ffn", "norm_mix_2",
                                                               "norm_mlp_2", "norm_ple_2")], axis=1),
        "convw": np.ascontiguousarray(g["conv_w"][0].reshape(4, 4, 128).transpose(2, 1, 0)),
        "convb": cols(g["conv_b"][0], 4),
        "bif": np.stack([g["b_igate"][0], g["b_fgate"][0]], axis=1),
        "sinks": g["sinks"][0], "gmh": g["g_mhead"][0], "gffn": g["g_ffn"][0], "gfin": g["g_final"],
        "ggn": g["gla_out_norm_2"].reshape(-1),
        "sk": np.ascontiguousarray(np.stack([g["sub_keys1"][0].T, g["sub_keys2"][0].T], axis=1)),
        "thin": np.ascontiguousarray(thin.reshape(8, 128, 24).transpose(1, 0, 2)),
        "gw2": g["gla_gate_w2_2"][0], "gb2": cols(g["gla_gate_b_2"][0], 4),
        "bqk": np.stack([g["moba_q_norm_2"][0], g["moba_k_norm_2"][0]], axis=1),
        "ex": np.concatenate([g["expert_down"][0], g["expert_up"][0]], axis=1),
        "pT": np.ascontiguousarray(g["p_2"][0, 0].T.reshape(2, 128, 256).transpose(1, 0, 2)),
        "wple": np.ascontiguousarray(g["w_ple_2"][0].reshape(2, 128, 1024).transpose(1, 0, 2)).reshape(128, 2048),
    }


def kernel(**inputs):
    import concourse.bacc as _bacc
    from concourse.bass_utils import run_bass_kernel_spmd as _run

    arrays = layout(inputs)
    nc = _bacc.Bacc("TRN2", target_bir_lowering=False, num_devices=1)
    A = {n: nc.dram_tensor(f"in_{n}", a.shape, F32, kind="ExternalInput").ap() for n, a in arrays.items()}
    out = nc.dram_tensor("out_0", (256, 1024), F32, kind="ExternalOutput").ap()
    program(nc, A, out)
    r = _run(nc, [{f"in_{n}": a for n, a in arrays.items()}], core_ids=[0])
    return r.results[0]["out_0"].reshape(1, 256, 1024)
```
